# Optimizing a Trainium2 kernel written in Bass

```python
import math
import jax
import jax.numpy as jnp
from jax import lax
import numpy as np
import jax, jax.numpy as jnp

D_MODEL = 1024
BATCH = 1
SEQ = 256
DEPTH = 2

PLE_DIM = 256
D_FF = 2816
LN_EPS = 1e-5
DEEPNORM_ALPHA = (2 * DEPTH) ** 0.25
DEEPNORM_BETA = (8 * DEPTH) ** -0.25
MACARON_W = 0.5

RW_HEADS = 8
RW_HEAD = 64
RW_WIDTH = RW_HEADS * RW_HEAD
RW_DECAY_LORA = 64
RW_AAA_LORA = 64
RW_GATE_LORA = 160
RW_GN_EPS = 1e-5 * RW_HEAD

GLA_HEADS = 4
GLA_DK = 64
GLA_DV = 128
GLA_GATE_LORA = 16
GLA_GATE_NORM = 16.0
GLA_CHUNK = 64

GDN_HEADS = 4
GDN_DK = 128
GDN_DV = 128
GDN_CONV = 4
GDN_CHUNK = 64

HEAD_NORM_EPS = 1e-6
L2_EPS = 1e-6
N_BRANCH = 3
BRANCH_WIDTH = 512

RW_SPLITS = (RW_WIDTH, RW_WIDTH, RW_WIDTH, RW_DECAY_LORA, RW_AAA_LORA, RW_GATE_LORA)
GLA_SPLITS = (GLA_HEADS * GLA_DK, GLA_HEADS * GLA_DK, GLA_HEADS * GLA_DV, GLA_GATE_LORA, GLA_HEADS * GLA_DV)
GDN_QKV = GDN_HEADS * (2 * GDN_DK + GDN_DV)
GDN_SPLITS = (GDN_QKV, GDN_HEADS, GDN_HEADS, GDN_HEADS * GDN_DV)
RW_IN = sum(RW_SPLITS)
GROUP_SPLITS = (RW_IN, sum(GLA_SPLITS), sum(GDN_SPLITS), N_BRANCH * D_MODEL)
D_IN = sum(GROUP_SPLITS)


def _split(h, sizes):
    idx, s = [], 0
    for w in sizes[:-1]:
        s += w
        idx.append(s)
    return jnp.split(h, idx, axis=-1)

def _heads(t, h, d):
    return t.reshape(t.shape[:-1] + (h, d))

def _layer_norm(x, g, b):
    xf = x.astype(jnp.float32)
    m = jnp.mean(xf, -1, keepdims=True)
    var = jnp.mean(jnp.square(xf - m), -1, keepdims=True)
    return ((xf - m) * lax.rsqrt(var + LN_EPS) * g + b).astype(x.dtype)

def _rms_norm(x, g):
    return x * lax.rsqrt(jnp.mean(jnp.square(x), -1, keepdims=True) + HEAD_NORM_EPS) * g

def _l2norm(x):
    return x * lax.rsqrt(jnp.sum(jnp.square(x), -1, keepdims=True) + L2_EPS)

def _swiglu(x, w1, w3, w2):
    return (jax.nn.silu(x @ w1) * (x @ w3)) @ w2

def rwkv7_time_mix(h_rw, mu, w0, w2, a0, a2, g2, k_k, k_a, r_k, gn_g, gn_b):
    B, T, _ = h_rw.shape
    prev = jnp.pad(h_rw, ((0, 0), (1, 0), (0, 0)))[:, :-1]
    h_rw = h_rw + (prev - h_rw) * mu
    r, k, v, w_lo, a_lo, g_lo = _split(h_rw, RW_SPLITS)
    w = -jax.nn.softplus(-(w0 + jnp.tanh(w_lo) @ w2)) - 0.5
    decay = jnp.exp(-jnp.exp(w))
    a = jax.nn.sigmoid(a0 + a_lo @ a2)
    g = jax.nn.sigmoid(g_lo) @ g2
    kk = _l2norm(_heads(k * k_k, RW_HEADS, RW_HEAD))
    k = k * (1.0 + (a - 1.0) * k_a)
    r, k, v, decay, a = (_heads(t, RW_HEADS, RW_HEAD) for t in (r, k, v, decay, a))

    def step(S, inp):
        r_t, k_t, v_t, d_t, a_t, b_t = inp
        sa = jnp.einsum('bhvk,bhk->bhv', S, a_t)
        S = S * d_t[:, :, None, :] + sa[..., None] * b_t[:, :, None, :] + v_t[..., None] * k_t[:, :, None, :]
        return S, jnp.einsum('bhvk,bhk->bhv', S, r_t)

    xs = tuple(jnp.moveaxis(t, 1, 0) for t in (r, k, v, decay, -kk, kk * a))
    S0 = jnp.zeros((B, RW_HEADS, RW_HEAD, RW_HEAD), jnp.float32)
    _, y = lax.scan(step, S0, xs)
    y = jnp.moveaxis(y, 0, 1)
    ym = jnp.mean(y, -1, keepdims=True)
    yv = jnp.mean(jnp.square(y - ym), -1, keepdims=True)
    y = ((y - ym) * lax.rsqrt(yv + RW_GN_EPS)).reshape(B, T, RW_WIDTH) * gn_g + gn_b
    bonus = jnp.sum(r * k * r_k, -1, keepdims=True) * v
    return (y + bonus.reshape(B, T, RW_WIDTH)) * g

def gla_mix(q, k, v, gk_lo, gate, gk_w2, gk_b, norm_g):
    B, T, _ = q.shape
    C, n, H = GLA_CHUNK, T // GLA_CHUNK, GLA_HEADS
    log_a = jax.nn.log_sigmoid(gk_lo @ gk_w2 + gk_b) / GLA_GATE_NORM

    def chunked(t, d):
        return t.reshape(B, n, C, H, d).transpose(1, 0, 3, 2, 4)

    q = chunked(q * GLA_DK ** -0.5, GLA_DK)
    k = chunked(k, GLA_DK)
    v = chunked(v, GLA_DV)
    b = jnp.cumsum(chunked(log_a, GLA_DK), axis=3)
    causal = jnp.tril(jnp.ones((C, C), dtype=bool))[:, :, None]

    def step(S, inp):
        q_c, k_c, v_c, b_c = inp
        rel = jnp.where(causal, b_c[:, :, :, None, :] - b_c[:, :, None, :, :], -jnp.inf)
        att = jnp.sum(q_c[:, :, :, None, :] * k_c[:, :, None, :, :] * jnp.exp(rel), axis=-1)
        o = att @ v_c + (q_c * jnp.exp(b_c)) @ S
        b_end = b_c[:, :, -1:, :]
        S = S * jnp.exp(b_end[:, :, 0, :, None]) + jnp.einsum('bhjd,bhjv->bhdv', k_c * jnp.exp(b_end - b_c), v_c)
        return S, o

    S0 = jnp.zeros((B, H, GLA_DK, GLA_DV), jnp.float32)
    _, o = lax.scan(step, S0, (q, k, v, b))
    o = o.transpose(1, 0, 3, 2, 4).reshape(B, T, H, GLA_DV)
    return _rms_norm(o, norm_g).reshape(B, T, H * GLA_DV) * jax.nn.silu(gate)

def gated_deltanet_mix(qkv, a_in, b_in, gate, conv_w, a_log, dt_bias, norm_g):
    B, T, _ = qkv.shape
    C, n, H = GDN_CHUNK, T // GDN_CHUNK, GDN_HEADS
    qkv = jax.nn.silu(lax.conv_general_dilated(
        qkv, conv_w[:, None, :].astype(qkv.dtype), (1,), [(GDN_CONV - 1, 0)],
        dimension_numbers=('NWC', 'WIO', 'NWC'), feature_group_count=qkv.shape[-1]))
    q, k, v = _split(qkv, (H * GDN_DK, H * GDN_DK, H * GDN_DV))
    q = _l2norm(_heads(q, H, GDN_DK)) * GDN_DK ** -0.5
    k = _l2norm(_heads(k, H, GDN_DK))
    v = _heads(v, H, GDN_DV)
    beta = jax.nn.sigmoid(b_in)
    g = -jnp.exp(a_log) * jax.nn.softplus(a_in + dt_bias)

    def chunked(t):
        t = jnp.moveaxis(t, 2, 1)
        return t.reshape((B, H, n, C) + t.shape[3:])

    q, k, v, beta, g = (chunked(t) for t in (q, k, v, beta, g))
    g = jnp.cumsum(g, axis=-1)
    causal = jnp.tril(jnp.ones((C, C), dtype=bool))
    strict = jnp.tril(jnp.ones((C, C), dtype=bool), -1)
    decay = jnp.exp(jnp.where(causal, g[..., :, None] - g[..., None, :], -jnp.inf))
    kb = k * beta[..., None]
    lower = jnp.where(strict, jnp.einsum('bhnid,bhnjd->bhnij', kb, k) * decay, 0.0)
    eye = jnp.eye(C, dtype=lower.dtype)
    t_inv = lax.linalg.triangular_solve(eye + lower, jnp.broadcast_to(eye, lower.shape),
                                        left_side=True, lower=True)
    u = t_inv @ (v * beta[..., None])
    w = t_inv @ (kb * jnp.exp(g)[..., None])
    att = jnp.einsum('bhnid,bhnjd->bhnij', q, k) * decay
    xs = tuple(jnp.moveaxis(t, 2, 0) for t in (q, k, u, w, g, att))

    def step(S, inp):
        q_c, k_c, u_c, w_c, g_c, att_c = inp
        v_new = u_c - w_c @ S
        o = (q_c * jnp.exp(g_c)[..., None]) @ S + att_c @ v_new
        g_end = g_c[..., -1:]
        S = S * jnp.exp(g_end)[..., None] + jnp.einsum('bhcd,bhcv->bhdv', k_c * jnp.exp(g_end - g_c)[..., None], v_new)
        return S, o

    S0 = jnp.zeros((B, H, GDN_DK, GDN_DV), jnp.float32)
    _, o = lax.scan(step, S0, xs)
    o = o.transpose(1, 0, 3, 2, 4).reshape(B, T, H, GDN_DV)
    return _rms_norm(o, norm_g).reshape(B, T, H * GDN_DV) * jax.nn.silu(gate)

def token_mixing(x, w_in, rw_mu, rw_w0, rw_w2, rw_a0, rw_a2, rw_g2, rw_k_k, rw_k_a, rw_r_k, rw_gn_g, rw_gn_b,
                 gla_gk_w2, gla_gk_b, gla_norm_g, gdn_conv_w, gdn_a_log, gdn_dt_bias, gdn_norm_g, w_branch, w_o):
    B, T, _ = x.shape
    h = (x @ w_in).astype(jnp.float32)
    h_rw, h_gla, h_gdn, h_gate = _split(h, GROUP_SPLITS)
    o_rw = rwkv7_time_mix(h_rw, rw_mu, rw_w0, rw_w2, rw_a0, rw_a2, rw_g2, rw_k_k, rw_k_a, rw_r_k, rw_gn_g, rw_gn_b)
    o_gla = gla_mix(*_split(h_gla, GLA_SPLITS), gla_gk_w2, gla_gk_b, gla_norm_g)
    o_gdn = gated_deltanet_mix(*_split(h_gdn, GDN_SPLITS), gdn_conv_w, gdn_a_log, gdn_dt_bias, gdn_norm_g)
    branches = jnp.stack([o_rw, o_gla, o_gdn], axis=2)
    proj = jnp.einsum('btnc,ncd->btnd', branches, w_branch)
    gates = jax.nn.sigmoid(h_gate).reshape(B, T, N_BRANCH, D_MODEL)
    merged = jnp.sum(gates * proj, axis=2)
    return merged.astype(x.dtype) @ w_o

def first_inputs(seed: int = 0) -> dict:
    key = jax.random.key(seed)
    ks = iter(jax.random.split(key, 40))
    L, D = DEPTH, D_MODEL
    bt = DEEPNORM_BETA

    def nrm(shape, scale):
        return jax.random.normal(next(ks), shape, jnp.float32) * scale

    def uni(shape, lo, hi):
        return jax.random.uniform(next(ks), shape, jnp.float32, lo, hi)

    dt = jnp.exp(uni((L, GDN_HEADS), math.log(1e-3), math.log(1e-1)))
    return {
        "x": nrm((BATCH, SEQ, D), 1.0),
        "p": nrm((L, BATCH, SEQ, PLE_DIM), 1.0),
        "ln_g": 1.0 + nrm((L, 4, D), 0.02),
        "ln_b": nrm((L, 4, D), 0.02),
        "ffn_w1": nrm((L, 2, D, D_FF), D ** -0.5),
        "ffn_w3": nrm((L, 2, D, D_FF), D ** -0.5),
        "ffn_w2": nrm((L, 2, D_FF, D), bt * D_FF ** -0.5),
        "w_in": nrm((L, D, D_IN), D ** -0.5),
        "rw_mu": uni((L, RW_IN), 0.0, 1.0),
        "rw_w0": uni((L, RW_WIDTH), -6.0, -1.0),
        "rw_w2": nrm((L, RW_DECAY_LORA, RW_WIDTH), 0.5 * RW_DECAY_LORA ** -0.5),
        "rw_a0": nrm((L, RW_WIDTH), 0.1),
        "rw_a2": nrm((L, RW_AAA_LORA, RW_WIDTH), 0.5 * RW_AAA_LORA ** -0.5),
        "rw_g2": nrm((L, RW_GATE_LORA, RW_WIDTH), RW_GATE_LORA ** -0.5),
        "rw_k_k": 0.85 + nrm((L, RW_WIDTH), 0.05),
        "rw_k_a": 1.0 + nrm((L, RW_WIDTH), 0.05),
        "rw_r_k": nrm((L, RW_HEADS, RW_HEAD), 0.1),
        "rw_gn_g": 1.0 + nrm((L, RW_WIDTH), 0.02),
        "rw_gn_b": nrm((L, RW_WIDTH), 0.02),
        "gla_gk_w2": nrm((L, GLA_GATE_LORA, GLA_HEADS * GLA_DK), GLA_GATE_LORA ** -0.5),
        "gla_gk_b": uni((L, GLA_HEADS * GLA_DK), 0.0, 3.0),
        "gla_norm_g": 1.0 + nrm((L, GLA_DV), 0.02),
        "gdn_conv_w": nrm((L, GDN_CONV, GDN_QKV), GDN_CONV ** -0.5),
        "gdn_a_log": jnp.log(uni((L, GDN_HEADS), 1.0, 16.0)),
        "gdn_dt_bias": dt + jnp.log(-jnp.expm1(-dt)),
        "gdn_norm_g": 1.0 + nrm((L, GDN_DV), 0.02),
        "w_branch": nrm((L, N_BRANCH, BRANCH_WIDTH, D), bt * BRANCH_WIDTH ** -0.5),
        "w_o": nrm((L, D, D), bt * D ** -0.5),
        "ple_w_gate": nrm((L, D, D), D ** -0.5),
        "ple_w_proj": nrm((L, PLE_DIM, D), bt * PLE_DIM ** -0.5),
    }

def first_block(x, p, ln_g, ln_b, ffn_w1, ffn_w3, ffn_w2, w_in, rw_mu, rw_w0, rw_w2, rw_a0, rw_a2, rw_g2,
              rw_k_k, rw_k_a, rw_r_k, rw_gn_g, rw_gn_b, gla_gk_w2, gla_gk_b, gla_norm_g, gdn_conv_w, gdn_a_log,
              gdn_dt_bias, gdn_norm_g, w_branch, w_o, ple_w_gate, ple_w_proj):
    a = DEEPNORM_ALPHA
    for i in range(DEPTH):
        x = _layer_norm(a * x + MACARON_W * _swiglu(x, ffn_w1[i, 0], ffn_w3[i, 0], ffn_w2[i, 0]), ln_g[i, 0], ln_b[i, 0])
        mix = token_mixing(x, w_in[i], rw_mu[i], rw_w0[i], rw_w2[i], rw_a0[i], rw_a2[i], rw_g2[i], rw_k_k[i],
                           rw_k_a[i], rw_r_k[i], rw_gn_g[i], rw_gn_b[i], gla_gk_w2[i], gla_gk_b[i], gla_norm_g[i],
                           gdn_conv_w[i], gdn_a_log[i], gdn_dt_bias[i], gdn_norm_g[i], w_branch[i], w_o[i])
        x = _layer_norm(a * x + mix, ln_g[i, 1], ln_b[i, 1])
        x = _layer_norm(a * x + MACARON_W * _swiglu(x, ffn_w1[i, 1], ffn_w3[i, 1], ffn_w2[i, 1]), ln_g[i, 2], ln_b[i, 2])
        ple = jax.nn.sigmoid(x @ ple_w_gate[i]) * (p[i] @ ple_w_proj[i])
        x = _layer_norm(a * x + ple, ln_g[i, 3], ln_b[i, 3])
    return x


GRID_W = 64
CTX_LEN = 256
N_MIXERS = 2
NORM_EPS = 1e-6
ATTN_HEADS = 16
ATTN_KV_HEADS = 4
HEAD_DIM = D_MODEL // ATTN_HEADS
ATTN_GROUP = ATTN_HEADS // ATTN_KV_HEADS
Q_WIDTH = ATTN_HEADS * HEAD_DIM
KV_WIDTH = ATTN_KV_HEADS * HEAD_DIM
QKV_WIDTH = Q_WIDTH + 2 * KV_WIDTH
AXIS_DIM = HEAD_DIM // 2
ROPE_THETA = 10000.0
Q_BLOCK = 128
HGRN_WIDTH = D_MODEL
HGRN_EXPAND = 128
HGRN_HEADS = HGRN_WIDTH // HGRN_EXPAND
HGRN_DK = HGRN_EXPAND
HGRN_DV = HGRN_WIDTH // HGRN_HEADS
HGRN_CHUNK = 64
FFN_HIDDEN = ((8 * D_MODEL // 3 + 255) // 256) * 256
N_ATTN_LAYERS = (DEPTH + 1) // 2
N_HGRN_LAYERS = DEPTH // 2


def rms_norm(x, w):
    xf = x.astype(jnp.float32)
    y = xf * lax.rsqrt(jnp.mean(xf * xf, axis=-1, keepdims=True) + NORM_EPS)
    return (y * w.astype(jnp.float32)).astype(x.dtype)

def modulate(h, shift, scale):
    return h * (1.0 + scale) + shift

def axial_rope_tables(n_tokens):
    rows = n_tokens // GRID_W
    row_pos = jnp.repeat(jnp.arange(rows), GRID_W).astype(jnp.float32)
    col_pos = jnp.tile(jnp.arange(GRID_W), rows).astype(jnp.float32)
    inv_freq = ROPE_THETA ** (-(jnp.arange(AXIS_DIM // 2, dtype=jnp.float32) * 2.0 / AXIS_DIM))
    ang_r = row_pos[:, None] * inv_freq
    ang_c = col_pos[:, None] * inv_freq
    return (jnp.cos(ang_r), jnp.sin(ang_r), jnp.cos(ang_c), jnp.sin(ang_c))

def rotate_half(x, cos, sin):
    x1, x2 = jnp.split(x, 2, axis=-1)
    return jnp.concatenate([x1 * cos - x2 * sin, x2 * cos + x1 * sin], axis=-1)

def apply_axial_rope(x, rope):
    cos_r, sin_r, cos_c, sin_c = rope
    xf = x.astype(jnp.float32)
    xr, xc = jnp.split(xf, 2, axis=-1)
    out = jnp.concatenate([rotate_half(xr, cos_r, sin_r), rotate_half(xc, cos_c, sin_c)], axis=-1)
    return out.astype(x.dtype)

def gqa_attend(q, k, v):
    s = jnp.einsum('bkgqd,bksd->bkgqs', q, k, preferred_element_type=jnp.float32) * (HEAD_DIM ** -0.5)
    p = jax.nn.softmax(s, axis=-1).astype(v.dtype)
    return jnp.einsum('bkgqs,bksd->bkgqd', p, v)

def attention_mixer(h_lat, h_ctx, w_qkv, q_norm, k_norm, w_o, rope, with_ctx_out):
    b, n, _ = h_lat.shape
    m = h_ctx.shape[1]
    w_q, w_kv = w_qkv[:, :Q_WIDTH], w_qkv[:, Q_WIDTH:]

    def queries(h):
        t = h.shape[1]
        q = (h @ w_q).reshape(b, t, ATTN_KV_HEADS, ATTN_GROUP, HEAD_DIM).transpose(0, 2, 3, 1, 4)
        return rms_norm(q, q_norm)

    def keys_values(h):
        t = h.shape[1]
        k, v = jnp.split(h @ w_kv, 2, axis=-1)
        k = k.reshape(b, t, ATTN_KV_HEADS, HEAD_DIM).transpose(0, 2, 1, 3)
        v = v.reshape(b, t, ATTN_KV_HEADS, HEAD_DIM).transpose(0, 2, 1, 3)
        return rms_norm(k, k_norm), v

    q_l = apply_axial_rope(queries(h_lat), rope)
    k_l, v_l = keys_values(h_lat)
    k_l = apply_axial_rope(k_l, rope)
    k_c, v_c = keys_values(h_ctx)
    k_all = jnp.concatenate([k_c, k_l], axis=2)
    v_all = jnp.concatenate([v_c, v_l], axis=2)

    nb = n // Q_BLOCK
    q_blocks = q_l.reshape(b, ATTN_KV_HEADS, ATTN_GROUP, nb, Q_BLOCK, HEAD_DIM).transpose(3, 0, 1, 2, 4, 5)
    o_blocks = lax.map(lambda qb: gqa_attend(qb, k_all, v_all), q_blocks)
    o_l = o_blocks.transpose(1, 0, 4, 2, 3, 5).reshape(b, n, Q_WIDTH)
    y_l = o_l @ w_o
    if not with_ctx_out:
        return y_l, None
    o_c = gqa_attend(queries(h_ctx), k_c, v_c)
    y_c = o_c.transpose(0, 3, 1, 2, 4).reshape(b, m, Q_WIDTH) @ w_o
    return y_l, y_c

def hgrn2_chunk_scan(q, k, log_f, v, s0):
    b, h, n, dk = q.shape
    dv = v.shape[-1]
    nc = n // HGRN_CHUNK

    def to_chunks(a):
        return a.reshape(b, h, nc, HGRN_CHUNK, a.shape[-1]).transpose(2, 0, 1, 3, 4)

    mask = jnp.tril(jnp.ones((HGRN_CHUNK, HGRN_CHUNK), dtype=bool))[None, None, :, :, None]

    def step(state, inp):
        qc, kc, gc, vc = inp
        L = jnp.cumsum(gc, axis=2)
        o_inter = jnp.einsum('bhtk,bhkv->bhtv', qc * jnp.exp(L), state)
        diff = L[:, :, :, None, :] - L[:, :, None, :, :]
        decay = jnp.where(mask, jnp.exp(jnp.where(mask, diff, 0.0)), 0.0)
        a = jnp.einsum('bhtk,bhtsk,bhsk->bhts', qc, decay, kc)
        o_intra = jnp.einsum('bhts,bhsv->bhtv', a, vc)
        L_end = L[:, :, -1:, :]
        new_state = jnp.exp(L_end[:, :, 0, :])[..., None] * state + jnp.einsum(
            'bhsk,bhsv->bhkv', kc * jnp.exp(L_end - L), vc)
        return new_state, o_inter + o_intra

    s_final, o = lax.scan(step, s0, (to_chunks(q), to_chunks(k), to_chunks(log_f), to_chunks(v)))
    return o.transpose(1, 2, 0, 3, 4).reshape(b, h, n, dv), s_final

def hgrn2_final_state(k, log_f, v):
    L = jnp.cumsum(log_f, axis=2)
    return jnp.einsum('bhsk,bhsv->bhkv', k * jnp.exp(L[:, :, -1:, :] - L), v)

def hgrn2_mixer(h_lat, h_ctx, w_in, lb, out_norm, w_o, with_ctx_out):
    b = h_lat.shape[0]

    def heads(a):
        return a.reshape(b, a.shape[1], HGRN_HEADS, -1).transpose(0, 2, 1, 3).astype(jnp.float32)

    def gates(z):
        f = lb + (1.0 - lb) * jax.nn.sigmoid(z.astype(jnp.float32))
        return heads(jnp.log(f)), heads(1.0 - f)

    def recurrent_inputs(h):
        z_fw, z_bw, v = jnp.split(h @ w_in[:, 2 * HGRN_WIDTH:], 3, axis=-1)
        g_fw, k_fw = gates(z_fw)
        g_bw, k_bw = gates(z_bw)
        return g_fw, k_fw, g_bw, k_bw, heads(v)

    def query_gate(h):
        q, g = jnp.split(h @ w_in[:, :2 * HGRN_WIDTH], 2, axis=-1)
        return heads(q), g

    def flip(a):
        return jnp.flip(a, axis=2)

    def readout(o, g):
        t = o.shape[2]
        o = rms_norm(o.transpose(0, 2, 1, 3), out_norm.reshape(HGRN_HEADS, HGRN_DV))
        o = o * jax.nn.sigmoid(g.astype(jnp.float32)).reshape(b, t, HGRN_HEADS, HGRN_DV)
        return o.reshape(b, t, HGRN_WIDTH).astype(h_lat.dtype) @ w_o

    zeros = jnp.zeros((b, HGRN_HEADS, HGRN_DK, HGRN_DV), jnp.float32)
    gc_fw, kc_fw, gc_bw, kc_bw, vc = recurrent_inputs(h_ctx)
    y_c = None
    if with_ctx_out:
        qc, gate_c = query_gate(h_ctx)
        oc_fw, s_fw = hgrn2_chunk_scan(qc, kc_fw, gc_fw, vc, zeros)
        oc_bw, s_bw = hgrn2_chunk_scan(flip(qc), flip(kc_bw), flip(gc_bw), flip(vc), zeros)
        y_c = readout(oc_fw + flip(oc_bw), gate_c)
    else:
        s_fw = hgrn2_final_state(kc_fw, gc_fw, vc)
        s_bw = hgrn2_final_state(flip(kc_bw), flip(gc_bw), flip(vc))

    q, gate = query_gate(h_lat)
    g_fw, k_fw, g_bw, k_bw, v = recurrent_inputs(h_lat)
    o_fw, _ = hgrn2_chunk_scan(q, k_fw, g_fw, v, s_fw)
    o_bw, _ = hgrn2_chunk_scan(flip(q), flip(k_bw), flip(g_bw), flip(v), s_bw)
    return readout(o_fw + flip(o_bw), gate), y_c

def swiglu(h, w_in, w_out):
    a, u = jnp.split(h @ w_in, 2, axis=-1)
    return (jax.nn.silu(a) * u) @ w_out

def second_inputs(seed: int = 0) -> dict:
    key = jax.random.key(seed)
    ks = jax.random.split(key, 19)
    D = D_MODEL

    def nrm(k, shape, scale):
        return jax.random.normal(k, shape, jnp.float32) * scale

    return {
        'x': nrm(ks[0], (BATCH, SEQ, D), 1.0),
        'c': nrm(ks[1], (BATCH, D), 1.0),
        'ctx': nrm(ks[2], (BATCH, CTX_LEN, D), 1.0),
        'c_ctx': nrm(ks[3], (D,), 1.0),
        'ada_w': nrm(ks[4], (DEPTH, D, 6 * D), 0.5 * D ** -0.5),
        'ada_b': nrm(ks[5], (DEPTH, 6 * D), 0.02),
        'norm_mix_w': 1.0 + nrm(ks[6], (DEPTH, D), 0.05),
        'norm_ffn_w': 1.0 + nrm(ks[7], (DEPTH, D), 0.05),
        'attn_w_qkv': nrm(ks[8], (N_ATTN_LAYERS, D, QKV_WIDTH), D ** -0.5),
        'attn_q_norm': 1.0 + nrm(ks[9], (N_ATTN_LAYERS, HEAD_DIM), 0.05),
        'attn_k_norm': 1.0 + nrm(ks[10], (N_ATTN_LAYERS, HEAD_DIM), 0.05),
        'attn_w_o': nrm(ks[11], (N_ATTN_LAYERS, Q_WIDTH, D), Q_WIDTH ** -0.5),
        'hgrn_w_in': nrm(ks[12], (N_HGRN_LAYERS, D, 5 * HGRN_WIDTH), D ** -0.5),
        'hgrn_lb_logits': nrm(ks[13], (DEPTH, HGRN_WIDTH), 0.5),
        'hgrn_out_norm': 1.0 + nrm(ks[14], (N_HGRN_LAYERS, HGRN_WIDTH), 0.05),
        'hgrn_w_o': nrm(ks[15], (N_HGRN_LAYERS, HGRN_WIDTH, D), HGRN_WIDTH ** -0.5),
        'ffn_w_in': nrm(ks[16], (DEPTH, D, 2 * FFN_HIDDEN), D ** -0.5),
        'ffn_w_out': nrm(ks[17], (DEPTH, FFN_HIDDEN, D), FFN_HIDDEN ** -0.5),
        'final_norm_w': 1.0 + nrm(ks[18], (D,), 0.05),
    }

def second_block(x, c, ctx, c_ctx, ada_w, ada_b, norm_mix_w, norm_ffn_w, attn_w_qkv, attn_q_norm,
              attn_k_norm, attn_w_o, hgrn_w_in, hgrn_lb_logits, hgrn_out_norm, hgrn_w_o,
              ffn_w_in, ffn_w_out, final_norm_w):
    n = x.shape[1]
    rope = axial_rope_tables(n)
    p = jax.nn.softmax(hgrn_lb_logits.astype(jnp.float32), axis=0)
    lower_bounds = jnp.cumsum(p, axis=0) - p[0:1]

    h, hc = x, ctx
    for i in range(DEPTH):
        last = i == DEPTH - 1
        mod_l = (jax.nn.silu(c) @ ada_w[i] + ada_b[i])[:, None, :]
        mod_c = (jax.nn.silu(c_ctx) @ ada_w[i] + ada_b[i])[None, None, :]
        sh1_l, sc1_l, gt1_l, sh2_l, sc2_l, gt2_l = jnp.split(mod_l, 6, axis=-1)
        sh1_c, sc1_c, gt1_c, sh2_c, sc2_c, gt2_c = jnp.split(mod_c, 6, axis=-1)

        hn_l = modulate(rms_norm(h, norm_mix_w[i]), sh1_l, sc1_l)
        hn_c = modulate(rms_norm(hc, norm_mix_w[i]), sh1_c, sc1_c)
        if i % N_MIXERS == 0:
            j = i // N_MIXERS
            y_l, y_c = attention_mixer(hn_l, hn_c, attn_w_qkv[j], attn_q_norm[j], attn_k_norm[j],
                                       attn_w_o[j], rope, not last)
        else:
            j = i // N_MIXERS
            y_l, y_c = hgrn2_mixer(hn_l, hn_c, hgrn_w_in[j], lower_bounds[i], hgrn_out_norm[j],
                                   hgrn_w_o[j], not last)

        h = h + gt1_l * y_l
        h = h + gt2_l * swiglu(modulate(rms_norm(h, norm_ffn_w[i]), sh2_l, sc2_l), ffn_w_in[i], ffn_w_out[i])
        if not last:
            hc = hc + gt1_c * y_c
            hc = hc + gt2_c * swiglu(modulate(rms_norm(hc, norm_ffn_w[i]), sh2_c, sc2_c),
                                     ffn_w_in[i], ffn_w_out[i])
    return rms_norm(h, final_norm_w)


def setup_inputs(seed=0):
    out = dict(first_inputs(seed))
    for name, value in second_inputs(seed + 1).items():
        if name != "x":
            out[name + "_2"] = value
    return out


def reference(
    x, p, ln_g, ln_b, ffn_w1, ffn_w3, ffn_w2, w_in, rw_mu, rw_w0, rw_w2, rw_a0, rw_a2, rw_g2,
    rw_k_k, rw_k_a, rw_r_k, rw_gn_g, rw_gn_b, gla_gk_w2, gla_gk_b, gla_norm_g, gdn_conv_w,
    gdn_a_log, gdn_dt_bias, gdn_norm_g, w_branch, w_o, ple_w_gate, ple_w_proj, c_2, ctx_2,
    c_ctx_2, ada_w_2, ada_b_2, norm_mix_w_2, norm_ffn_w_2, attn_w_qkv_2, attn_q_norm_2,
    attn_k_norm_2, attn_w_o_2, hgrn_w_in_2, hgrn_lb_logits_2, hgrn_out_norm_2, hgrn_w_o_2,
    ffn_w_in_2, ffn_w_out_2, final_norm_w_2,
):
    x = first_block(
        x, p, ln_g, ln_b, ffn_w1, ffn_w3, ffn_w2, w_in, rw_mu, rw_w0, rw_w2, rw_a0, rw_a2,
        rw_g2, rw_k_k, rw_k_a, rw_r_k, rw_gn_g, rw_gn_b, gla_gk_w2, gla_gk_b, gla_norm_g,
        gdn_conv_w, gdn_a_log, gdn_dt_bias, gdn_norm_g, w_branch, w_o, ple_w_gate, ple_w_proj,
    )
    return second_block(
        x, c_2, ctx_2, c_ctx_2, ada_w_2, ada_b_2, norm_mix_w_2, norm_ffn_w_2, attn_w_qkv_2,
        attn_q_norm_2, attn_k_norm_2, attn_w_o_2, hgrn_w_in_2, hgrn_lb_logits_2,
        hgrn_out_norm_2, hgrn_w_o_2, ffn_w_in_2, ffn_w_out_2, final_norm_w_2,
    )


_drawn_inputs = setup_inputs


def setup_inputs(seed=0):
    import zlib

    import numpy as np

    out = dict(_drawn_inputs(seed))
    spreads = {}
    factors = {'rw_w2': 8.0,
     'rw_a0': 8.0,
     'rw_a2': 3.638,
     'rw_k_k': 8.0,
     'rw_k_a': 8.0,
     'rw_r_k': 3.361,
     'rw_gn_g': 8.0,
     'rw_gn_b': 8.0,
     'gla_gk_w2': 8.0,
     'gla_norm_g': 8.0,
     'gdn_a_log': 3.57,
     'gdn_norm_g': 8.0,
     'ctx_2': 2.802,
     'norm_mix_w_2': 3.761,
     'attn_q_norm_2': 8.0,
     'attn_k_norm_2': 8.0,
     'hgrn_out_norm_2': 6.819,
     'norm_ffn_w_2': 3.311}
    for name, (base, spread) in spreads.items():
        noise = np.random.default_rng([zlib.crc32(name.encode()), seed]).standard_normal(out[name].shape)
        drawn = base * np.exp(spread * noise) if base else spread * noise
        out[name] = jnp.asarray(drawn.astype(out[name].dtype))
    for name, factor in factors.items():
        out[name] = (out[name] * factor).astype(out[name].dtype)
    return out
```

```python
from contextlib import ExitStack

import numpy as np
import concourse.bass as bass
from concourse import mybir

F32 = mybir.dt.float32
U32 = mybir.dt.uint32
ACT = mybir.ActivationFunctionType
ALU = mybir.AluOpType
AX = mybir.AxisListType

P = 128
D = 1024
KT = D // P
SEQ = 256
CTX = 256
DEPTH = 2
D_FF = 2816
FT = D_FF // P
LN_EPS = 1e-5
ALPHA = (2 * DEPTH) ** 0.25
C = 64
LEVELS = [1, 2, 4, 8, 16, 32]
RING = 3
PLE = 256
RWK_C = float(np.exp(-0.5))
HEAD_EPS = 1e-6
GRID_W = 64
ROPE_THETA = 10000.0
AXIS_DIM = 32


class Side:

    def __init__(self, eng):
        self.e, self.raised, self.seen = eng, {}, {}
        self.wait_ge, self.sem_inc = eng.wait_ge, eng.sem_inc

    def up(self, sem, n=1):
        self.raised[sem.name] = self.raised.get(sem.name, 0) + n
        return n

    def sent(self, sem):
        return self.raised[sem.name]

    def due(self, sem, n=1):
        self.seen[sem.name] = self.seen.get(sem.name, 0) + n
        return self.seen[sem.name]


class Banks:

    def __init__(self, banks, filled, freed):
        self.banks, self.filled, self.freed = banks, filled, freed
        self.opened = self.taken = 0

    def next_free(self):
        return self.opened + 1

    def free_bank(self):
        self.opened += 1
        return self.banks[(self.opened - 1) % len(self.banks)]

    def next_filled(self):
        return self.taken + 1

    def filled_bank(self):
        self.taken += 1
        return self.banks[(self.taken - 1) % len(self.banks)]


def constants():
    p, f = np.arange(P)[:, None], np.arange(P)[None, :]
    same = p // C == f // C
    parts = {"ident": p == f, "ones": np.ones((P, P)), "half_ones": same,
             "head_sel": p // C == np.arange(2)[None, :],
             "strictU": same & (f > p), "inclU": same & (f >= p)}
    def pair(h, right, left):
        return (right // (2 * h) == left // (2 * h)) & (right % (2 * h) >= h) & (left % (2 * h) < h)
    parts["lvlT"] = np.concatenate([pair(h, f, p) for h in LEVELS], 1)
    parts["lvl"] = np.concatenate([pair(h, p, f) for h in LEVELS], 1)
    parts["resets"] = np.ones((P, 1)) * (np.arange(SEQ)[None, :] % C != 0)
    tok = np.arange(SEQ)
    pos = np.stack([tok // GRID_W, tok % GRID_W], 1).astype(np.float32)
    freq = np.float32(ROPE_THETA) ** (-(np.arange(AXIS_DIM // 2, dtype=np.float32) * np.float32(2.0) / np.float32(AXIS_DIM)))
    ang = (pos[:, :, None] * freq).astype(np.float32)
    table = np.stack([np.cos(ang), np.sin(ang)], 1).reshape(SEQ // P, P, 2 * AXIS_DIM)
    parts["rope"] = table.transpose(1, 0, 2).reshape(P, -1)
    at, cols, n = {}, [], 0
    for name, m in parts.items():
        at[name] = (n, m.shape[1])
        cols.append(m.astype(np.float32))
        n += m.shape[1]
    at["causal2"] = (at["strictU"][0], 2 * P)
    return at, np.ascontiguousarray(np.concatenate(cols, 1))


CST_AT, CST = constants()
CST_COLS = CST.shape[1]


def two_blocks(nc, a, out):
    ctx = ExitStack()
    with ctx:
        def sb(name, shape, dt=F32):
            return ctx.enter_context(nc.sbuf_tensor(name, shape, dt))

        def sem(name):
            return ctx.enter_context(nc.semaphore(name))

        L_ready = sem("L_ready")
        PT_ready = sem("PT_ready")
        a_ready = sem("a_ready")
        act_bank_filled = sem("act_bank_filled")
        act_bank_freed = sem("act_bank_freed")
        act_step = sem("act_step")
        ada_ready = sem("ada_ready")
        ada_rows_ready = sem("ada_rows_ready")
        beta_ready = sem("beta_ready")
        bk_tok_ready = sem("bk_tok_ready")
        block_used = sem("block_used")
        bonus_in_ready = sem("bonus_in_ready")
        brT_ready = sem("brT_ready")
        branch_ready = sem("branch_ready")
        c_cols_ready = sem("c_cols_ready")
        c_landed = sem("c_landed")
        cols_free = sem("cols_free")
        cols_ready = sem("cols_ready")
        consts_landed = sem("consts_landed")
        conv_ready = sem("conv_ready")
        conv_silu_ready = sem("conv_silu_ready")
        ctx_decay_ready = sem("ctx_decay_ready")
        ctx_diff_ready = sem("ctx_diff_ready")
        ctx_keys_ready = sem("ctx_keys_ready")
        ctx_landed = sem("ctx_landed")
        ddecay_ready = sem("ddecay_ready")
        decay_ready = sem("decay_ready")
        diag_ready = sem("diag_ready")
        diff_ready = sem("diff_ready")
        dlog_ready = sem("dlog_ready")
        dnorm_in_ready = sem("dnorm_in_ready")
        dnorm_ready = sem("dnorm_ready")
        dss_ready = sem("dss_ready")
        dve_bank_filled = sem("dve_bank_filled")
        dve_bank_freed = sem("dve_bank_freed")
        dve_step = sem("dve_step")
        expL_ready = sem("expL_ready")
        final_norm_landed = sem("final_norm_landed")
        forget_ready = sem("forget_ready")
        gE_ready = sem("gE_ready")
        g_ready = sem("g_ready")
        gates_ready = sem("gates_ready")
        gates_used = sem("gates_used")
        gb_ready = sem("gb_ready")
        gdn_T_ready = sem("gdn_T_ready")
        gdn_in_ready = sem("gdn_in_ready")
        gk_abs_ready = sem("gk_abs_ready")
        gk_log_ready = sem("gk_log_ready")
        gla_in_ready = sem("gla_in_ready")
        head_std_ready = sem("head_std_ready")
        head_var_ready = sem("head_var_ready")
        hgrn_in_ready = sem("hgrn_in_ready")
        hidden_ready = sem("hidden_ready")
        kend_ready = sem("kend_ready")
        key_tok_ready = sem("key_tok_ready")
        lb_exp_ready = sem("lb_exp_ready")
        lb_max_ready = sem("lb_max_ready")
        lb_rows_landed = sem("lb_rows_landed")
        level_masked = sem("level_masked")
        level_product_ready = sem("level_product_ready")
        level_ready = sem("level_ready")
        ln_landed = sem("ln_landed")
        ln_used = sem("ln_used")
        lnp_free = sem("lnp_free")
        log_forget_ready = sem("log_forget_ready")
        lora_in_ready = sem("lora_in_ready")
        lora_landed = sem("lora_landed")
        lora_mixed = sem("lora_mixed")
        lora_used = sem("lora_used")
        max_ready = sem("max_ready")
        merged_ready = sem("merged_ready")
        mix_rows_landed = sem("mix_rows_landed")
        norm_ready = sem("norm_ready")
        oT_ready = sem("oT_ready")
        out_norm_landed = sem("out_norm_landed")
        out_norm_used = sem("out_norm_used")
        p_T_ready = sem("p_T_ready")
        p_landed = sem("p_landed")
        ple_ready = sem("ple_ready")
        pool_step = sem("pool_step")
        probs_ready = sem("probs_ready")
        probs_scaled = sem("probs_scaled")
        qkT_ready = sem("qkT_ready")
        qk_norm_landed = sem("qk_norm_landed")
        qk_ready = sem("qk_ready")
        qk_std_ready = sem("qk_std_ready")
        qk_tile_ready = sem("qk_tile_ready")
        qk_tile_turned = sem("qk_tile_turned")
        qk_var_ready = sem("qk_var_ready")
        qkv_ready = sem("qkv_ready")
        readout_ready = sem("readout_ready")
        result_ready = sem("result_ready")
        result_stored = sem("result_stored")
        rows2_landed = sem("rows2_landed")
        rows_landed = sem("rows_landed")
        rwkv_T_ready = sem("rwkv_T_ready")
        sa_ready = sem("sa_ready")
        silu_ready = sem("silu_ready")
        silu_used = sem("silu_used")
        softplus_in_ready = sem("softplus_in_ready")
        softplus_log_ready = sem("softplus_log_ready")
        solve_started = sem("solve_started")
        solved = sem("solved")
        sq_ready = sem("sq_ready")
        ss_ready = sem("ss_ready")
        state_ready = sem("state_ready")
        std_ready = sem("std_ready")
        sw_ready = sem("sw_ready")
        v_tok_ready = sem("v_tok_ready")
        var_ready = sem("var_ready")
        xT_ready = sem("xT_ready")
        x_landed = sem("x_landed")
        x_ready = sem("x_ready")
        x_rows_ready = sem("x_rows_ready")
        x_turned = sem("x_turned")
        xn_ready = sem("xn_ready")
        block_landed = [sem(f"block_landed{i}") for i in range(RING)]
        psum = [ctx.enter_context(nc.psum_tensor(f"bank{i}", [P, 512], F32)) for i in range(8)]
        to_dve = Banks(psum[:4], dve_bank_filled, dve_bank_freed)
        to_act = Banks(psum[4:], act_bank_filled, act_bank_freed)

        ring = sb("ring", [P, RING, 8, 512])
        xtok = sb("xtok", [P, 2, D])
        ctok = sb("ctok", [P, 2, D])
        xT = sb("xT", [P, KT, 512])
        lnp = sb("lnp", [P, 2, D])
        cst = sb("cst", [P, CST_COLS])

        def const(name):
            off, n = CST_AT[name]
            return cst[:, off:off + n]

        ident, ones, half_ones, head_sel = const("ident"), const("ones"), const("half_ones"), const("head_sel")
        inclU, strictU, causal2, resets = const("inclU"), const("strictU"), const("causal2"), const("resets")
        lvlT = const("lvlT").rearrange("p (l i) -> p l i", l=len(LEVELS))
        lvl = const("lvl").rearrange("p (l i) -> p l i", l=len(LEVELS))
        rows = sb("rows", [P, P])
        cols = sb("cols", [P, P])
        small = sb("small", [P, 64])
        stats = sb("stats", [P, 2, 6])
        gnp = sb("gnp", [P, 2, 512])
        normg = sb("normg", [P, 2, P])
        ab_par = sb("ab_par", [P, 2, 4])
        modp = sb("modp", [P, 304])
        rope = const("rope")
        arena_cols = (nc.sbuf_bytes_remaining - 64) // 4
        arena_cols -= arena_cols % 16
        arena = sb("arena", [P, arena_cols])

        def at(off, *shape):
            n = int(np.prod(shape))
            assert off + n <= arena_cols, (off, shape, arena_cols)
            v = arena[:, off:off + n]
            if len(shape) == 2:
                v = v.rearrange("p (a b) -> p a b", a=shape[0])
            if len(shape) == 3:
                v = v.rearrange("p (a b c) -> p a b c", a=shape[0], b=shape[1])
            if len(shape) == 4:
                v = v.rearrange("p (a b c d) -> p a b c d", a=shape[0], b=shape[1], c=shape[2])
            return v

        hid = arena[:, 0:FT * 512]
        silu_buf = at(FT * 512, 2, 512)

        block = ctx.enter_context(nc.Block())

        def k_rows(w, c0, n):
            return w.rearrange("(k p) n -> p k n", p=P)[:, :, c0:c0 + n]

        def sp_program(eng):
            sp = Side(eng)
            blocks = [0]

            def load(*parts):
                n = blocks[0]
                eng.wait_ge(block_used, sp.due(block_used))
                for k0, c0, src in parts:
                    kk, w = src.shape[1], src.shape[2]
                    if k0 is None:
                        dst = ring[:, n % RING].rearrange("p k n -> p (k n)")[:, 0:kk * w].rearrange(
                            "p (k n) -> p k n", n=w)
                    else:
                        dst = ring[:, n % RING, k0:k0 + kk, c0:c0 + w]
                    eng.dma_start(dst, src).then_inc(block_landed[n % RING], 16)
                blocks[0] += 1

            def ffn(w_gate, g0, w_up, u0, w_down):
                for b in range(FT // 2):
                    load((0, 0, k_rows(w_gate, g0 + 256 * b, 256)), (0, 256, k_rows(w_up, u0 + 256 * b, 256)))
                for half in range(2):
                    for k0 in range(0, FT, 8):
                        load((0, 0, k_rows(w_down, 512 * half, 512)[:, k0:min(k0 + 8, FT)]))

            def wide(w, c0, n):
                for c in range(c0, c0 + n, 512):
                    load((0, 0, k_rows(w, c, min(512, c0 + n - c))))

            first_loads(load, wide, ffn)
            second_loads(load, wide, ffn)
            eng.wait_ge(result_ready, 2)
            eng.dma_start(out[0].rearrange("(t p) d -> p t d", p=P), xtok[:]).then_inc(result_stored, 16)
            eng.wait_ge(result_stored, 16)

        W = a["w_in"]
        RW0, GLA0, GDN0, GATE0 = 0, 1824, 3376, 5432

        def first_loads(load, wide, ffn):
            ada = iter([(n // 12, n % 12 * 512) for n in range(DEPTH * 6 * D // 512)])

            def modulation():
                for _ in range(3):
                    l2, c0 = next(ada)
                    wide(a["ada_w_2"][l2], c0, 512)

            for l in range(DEPTH):
                ffn(a["ffn_w1"][l, 0], 0, a["ffn_w3"][l, 0], 0, a["ffn_w2"][l, 0])
                modulation()
                wide(W[l], 1536, 288)
                wide(W[l], 0, 1536)
                wide(W[l], GLA0, 1024)
                wide(W[l], GLA0 + 1040, 512)
                load((0, 0, k_rows(W[l], GLA0 + 1024, 16)), (0, 16, k_rows(W[l], GDN0 + 1536, 8)))
                wide(W[l], GDN0, 1536)
                wide(W[l], GDN0 + 1544, 512)
                for n in range(3):
                    wide(W[l], GATE0 + 1024 * n, 1024)
                    load((None, 0, k_rows(a["w_branch"][l, n], 0, 1024)))
                wide(a["w_o"][l], 0, 1024)
                modulation()
                ffn(a["ffn_w1"][l, 1], 0, a["ffn_w3"][l, 1], 0, a["ffn_w2"][l, 1])
                modulation()
                load((None, 0, k_rows(a["ple_w_proj"][l], 0, 1024)))
                wide(a["ple_w_gate"][l], 0, 1024)
                modulation()

        class Tensor(Side):

            def __init__(self, eng):
                super().__init__(eng)
                self.blocks = 0
                self.to_release = 0
                self.landed = {}

            def mm(self, o, lhsT, rhs, start=True, stop=True):
                return self.e.matmul(o, lhsT, rhs, start=start, stop=stop, skip_group_check=True)

            def turn(self, o, x, n=P):
                return self.e.transpose(o, x, ident[0:n, 0:n])

            def release(self, mm):
                if self.to_release:
                    self.to_release -= 1
                    mm.then_inc(block_used, 1)

            def block(self, parts=1):
                n = self.blocks % RING
                self.landed[n] = self.landed.get(n, 0) + 16 * parts
                self.wait_ge(block_landed[n], self.landed[n])
                self.blocks += 1
                return ring[:, n]

            def used(self):
                self.to_release += 1

        def pe_program(eng):
            pe = Tensor(eng)
            pe.sem_inc(block_used, pe.up(block_used, RING))
            pe.wait_ge(consts_landed, pe.due(consts_landed, 16))
            first_pe(pe)
            second_pe(pe)

        def pe_turn_x(pe, tts):
            for tt, src in tts:
                pe.wait_ge(x_ready, pe.due(x_ready))
                for q in range(2):
                    pe.wait_ge(to_act.freed, to_act.next_free())
                    bank = to_act.free_bank()
                    for k in range(4):
                        kt = 4 * q + k
                        mm = pe.turn(bank[:, k * P:(k + 1) * P], src[:, kt * P:(kt + 1) * P])
                        if k == 3:
                            mm.then_inc(to_act.filled, 1)

        def pe_T(pe, blk, banks, c0, widths, T=SEQ, x=None):
            x = xT if x is None else x
            per = 512 // T
            for g in range(0, len(widths), per):
                pe.wait_ge(banks.freed, banks.next_free())
                bank = banks.free_bank()
                mine = widths[g:g + per]
                for j, w in enumerate(mine):
                    for k in range(KT):
                        mm = pe.mm(bank[0:w, j * T:(j + 1) * T], blk[:, k, c0:c0 + w],
                                   x[:, k, 0:T], k == 0, k == KT - 1)
                        if j == k == 0:
                            pe.release(mm)
                        if j == len(mine) - 1 and k == KT - 1:
                            mm.then_inc(banks.filled, 1)
                    c0 += w

        def pe_tok(pe, blk, banks, c0, w, lhs, tts=(0, 1), K=KT, start=True, last=True, opened=None):
            if opened is None:
                opened = []
                for _ in tts:
                    pe.wait_ge(banks.freed, banks.next_free())
                    opened.append(banks.free_bank())
            for tt, bank in zip(tts, opened):
                for k in range(K):
                    mm = pe.mm(bank[:, 0:w], lhs(k, tt), blk[:, k, c0:c0 + w], start and k == 0, last and k == K - 1)
                    if k == 0:
                        pe.release(mm)
                    if last and k == K - 1:
                        mm.then_inc(banks.filled, 1)
            return opened

        def x_lhs(k, tt):
            return xT[:, k, tt * P:(tt + 1) * P]

        def hid_lhs(T):
            return lambda k, tt: hid[:, k * T + tt * P:k * T + (tt + 1) * P]

        def pe_ffn(pe, T):
            tts = tuple(range(T // P))
            pe.wait_ge(xT_ready, pe.due(xT_ready))
            for b in range(FT // 2):
                blk = pe.block(2)
                if T == SEQ:
                    pe_T(pe, blk, to_act, 0, [P, P], T)
                    pe_T(pe, blk, to_dve, 256, [P, P], T)
                else:
                    for j in range(2):
                        pe_T(pe, blk, to_act, j * P, [P], T)
                        pe_T(pe, blk, to_dve, 256 + j * P, [P], T)
                pe.used()
            pe.wait_ge(hidden_ready, pe.due(hidden_ready))
            for half in range(2):
                opened = None
                for k0 in range(0, FT, 8):
                    n = min(8, FT - k0)
                    blk = pe.block()
                    lhs = hid_lhs(T)
                    opened = pe_tok(pe, blk, to_dve, 0, 512, lambda k, tt: lhs(k0 + k, tt), tts, n, k0 == 0,
                                    k0 + n == FT, opened)
                    pe.used()

        def act_turn_x(act, tts):
            for tt, _ in tts:
                for q in range(2):
                    act.wait_ge(to_act.filled, to_act.next_filled())
                    bank = to_act.filled_bank()
                    ins = act.e.copy(xT[:, 4 * q:4 * q + 4, tt * P:(tt + 1) * P],
                                                      bank[:].rearrange("p (k t) -> p k t", k=4))
                    ins.then_inc(to_act.freed, act.up(to_act.freed))
                    act.wait_ge(to_act.freed, act.sent(to_act.freed))
                act.sem_inc(x_turned, act.up(x_turned))
            act.sem_inc(xT_ready, act.up(xT_ready))

        def act_ffn(act, T):
            for g in range(FT * T // 512):
                act.wait_ge(to_act.filled, to_act.next_filled())
                bank = to_act.filled_bank()
                act.wait_ge(silu_used, act.due(silu_used))
                ins = act.e.activation(silu_buf[:, act.silus % 2], bank[:], ACT.Silu)
                ins.then_inc(to_act.freed, act.up(to_act.freed))
                act.wait_ge(to_act.freed, act.sent(to_act.freed))
                act.sem_inc(silu_ready, act.up(silu_ready))
                act.silus += 1

        def dve_ffn(dve, T):
            v = nc.vector
            for g in range(FT * T // 512):
                dve.wait_ge(to_dve.filled, to_dve.next_filled())
                bank = to_dve.filled_bank()
                dve.wait_ge(silu_ready, dve.due(silu_ready))
                ins = v.tensor_tensor(hid[:, g * 512:(g + 1) * 512], bank[:],
                                                       silu_buf[:, dve.silus % 2], ALU.mult)
                ins.then_inc(to_dve.freed, dve.up(to_dve.freed))
                dve.wait_ge(to_dve.freed, dve.sent(to_dve.freed))
                dve.sem_inc(silu_used, dve.up(silu_used))
                dve.silus += 1
            dve.sem_inc(hidden_ready, dve.up(hidden_ready))

        def dve_residual(dve, scale):
            for half in range(2):
                for tt in range(2):
                    dve.wait_ge(to_dve.filled, to_dve.next_filled())
                    bank = to_dve.filled_bank()
                    x = xtok[:, tt, half * 512:(half + 1) * 512]
                    ins = nc.vector.scalar_tensor_tensor(
                              out=x, in0=bank[:], scalar=scale, in1=x, op0=ALU.mult, op1=ALU.add)
                    ins.then_inc(to_dve.freed, dve.up(to_dve.freed))
                    dve.wait_ge(to_dve.freed, dve.sent(to_dve.freed))

        def dve_layer_norm(dve, last=False):
            v = nc.vector
            dve.wait_ge(ln_landed, dve.due(ln_landed, 32))
            for tt in range(2):
                x = xtok[:, tt]
                for h in range(2):
                    v.bn_stats(stats[:, h], x[:, h * 512:(h + 1) * 512]).then_inc(dve_step, dve.up(dve_step))
                    dve.wait_ge(dve_step, dve.sent(dve_step))
                ins = v.bn_aggr(small[:, 0:2], stats[:].rearrange("p a b -> p (a b)"))
                ins.then_inc(dve_step, dve.up(dve_step))
                dve.wait_ge(dve_step, dve.sent(dve_step))
                ins = v.tensor_scalar(small[:, 2:3], small[:, 1:2], LN_EPS, None, ALU.add)
                ins.then_inc(var_ready, dve.up(var_ready))
                dve.wait_ge(var_ready, dve.sent(var_ready))
                dve.wait_ge(std_ready, dve.due(std_ready))
                v.reciprocal(small[:, 4:5], small[:, 3:4]).then_inc(dve_step, dve.up(dve_step))
                dve.wait_ge(dve_step, dve.sent(dve_step))
                ins = v.tensor_scalar(x, x, small[:, 0:1], small[:, 4:5], ALU.subtract, ALU.mult)
                ins.then_inc(dve_step, dve.up(dve_step))
                dve.wait_ge(dve_step, dve.sent(dve_step))
                v.tensor_tensor(x, x, lnp[:, 0], ALU.mult).then_inc(dve_step, dve.up(dve_step))
                dve.wait_ge(dve_step, dve.sent(dve_step))
                ready = dve_step if last else x_ready
                v.tensor_tensor(x, x, lnp[:, 1], ALU.add).then_inc(ready, dve.up(ready))
                dve.wait_ge(ready, dve.sent(ready))
            dve.sem_inc(ln_used, dve.up(ln_used))
            if not last:
                dve_scale_x(dve)

        def dve_scale_x(dve):
            for tt in range(2):
                dve.wait_ge(x_turned, dve.due(x_turned))
                ins = nc.vector.tensor_scalar(xtok[:, tt], xtok[:, tt], ALPHA, None, ALU.mult)
                ins.then_inc(dve_step, dve.up(dve_step))
                dve.wait_ge(dve_step, dve.sent(dve_step))

        def act_std(act, n=2):
            for _ in range(n):
                act.wait_ge(var_ready, act.due(var_ready))
                act.e.activation(small[:, 3:4], small[:, 2:3], ACT.Sqrt).then_inc(std_ready, act.up(std_ready))
                act.wait_ge(std_ready, act.sent(std_ready))

        X2 = [(0, xtok[:, 0]), (1, xtok[:, 1])]

        class Bump:

            def __init__(self, start):
                self.o = start

            def __call__(self, *shape):
                v = at(self.o, *shape)
                self.o += int(np.prod(shape))
                return v

        held = Bump(0)
        gla_qk = held(4, SEQ)
        gla_lo = held(SEQ)
        gla_z = held(2, SEQ)
        gla_v = held(2, 512)
        gla_gate = held(2, 512)
        gdn_T = held(12, SEQ)
        gdn_ab = held(2, 8)
        gdn_gate = held(2, 512)
        brT = held(4, SEQ)
        br_tok = held(2, 512)
        WORK = held.o
        merged = ctok
        lora_w = lnp[:, 0, 0:512]
        g2a = lnp[:, 0, 512:1024]
        g2b = lnp[0:32, 1, 0:512]
        gk2 = lnp[0:16, 1, 512:768]

        def gate_at(tt, half):
            k = 4 * tt + 2 * half
            return xT[:, k:k + 2, SEQ:512]

        MU, W0, A0, KKR, KAR, RKR, GKB, CONV, NROWS = 0, 15, 19, 23, 27, 31, 35, 37, 85
        OMKA = 88

        def pool_mix(pool, l):
            e = pool.e
            free_again = cols_free if l else c_cols_ready
            pool.wait_ge(free_again, pool.due(free_again))
            e.memset(rows[:], 0.0).then_inc(pool_step, pool.up(pool_step))
            pool.wait_ge(pool_step, pool.sent(pool_step))

            def row(r, v):
                n = v.shape[0] // P
                e.dma_start(rows[r:r + n, :], v.rearrange("(r p) -> r p", p=P)).then_inc(rows_landed, 16)

            row(MU, a["rw_mu"][l, 0:1792])
            e.dma_start(rows[MU + 14:MU + 15, 0:32], a["rw_mu"][l, 1792:1824].rearrange("(a n) -> a n", a=1)
                        ).then_inc(rows_landed, 16)
            row(W0, a["rw_w0"][l])
            row(A0, a["rw_a0"][l])
            row(KKR, a["rw_k_k"][l])
            row(KAR, a["rw_k_a"][l])
            row(RKR, a["rw_r_k"][l].rearrange("h d -> (h d)"))
            row(GKB, a["gla_gk_b"][l])
            e.dma_start(rows[CONV:CONV + 48, :], a["gdn_conv_w"][l].rearrange("i (r p) -> (i r) p", p=P)
                        ).then_inc(rows_landed, 16)
            for j, n in enumerate(("rw_gn_g", "rw_gn_b")):
                e.dma_start(gnp[:, j], a[n][l:l + 1, :].broadcast_to([P, 512])).then_inc(mix_rows_landed, 16)
            for j, n in enumerate(("gla_norm_g", "gdn_norm_g")):
                e.dma_start(normg[:, j], a[n][l:l + 1, :].broadcast_to([P, P])).then_inc(mix_rows_landed, 16)
            for j, n in enumerate(("gdn_a_log", "gdn_dt_bias")):
                e.dma_start(ab_par[:, j], a[n][l:l + 1, :].broadcast_to([P, 4])).then_inc(mix_rows_landed, 16)
            pool.wait_ge(ln_used, pool.due(ln_used))
            e.dma_start(lora_w[0:64, :], a["rw_w2"][l]).then_inc(lora_landed, 16)
            e.dma_start(lora_w[64:128, :], a["rw_a2"][l]).then_inc(lora_landed, 16)
            e.dma_start(g2a, a["rw_g2"][l, 0:128, :]).then_inc(lora_landed, 16)
            e.dma_start(g2b, a["rw_g2"][l, 128:160, :]).then_inc(lora_landed, 16)
            e.dma_start(gk2, a["gla_gk_w2"][l]).then_inc(lora_landed, 16)
            pool.wait_ge(lora_used, pool.due(lora_used))

        w = Bump(WORK)
        r_T = w(4, SEQ)
        vT = w(4, SEQ)
        loT = w(3, SEQ)
        sw = w(4, SEQ)
        eLx = w(4, SEQ)
        eiL = w(4, SEQ)
        sq = w(4, SEQ)
        PREP_END = w.o
        k_T = w(4, SEQ)
        eL = w(4, SEQ)
        bT = w(4, SEQ)
        AR = at(w.o, 4, 4, SEQ)
        w.o += 16 * SEQ
        v_tok = w(2, 512)
        g_tok = w(2, 512)
        bonus = small[:, 40:56]
        m = Bump(WORK)
        M4 = m(8, 4, P)
        Am = m(8, P)
        BKtok = m(2, 512)
        gn_tmp = m(512)
        Hst = m(4, 64)
        assert m.o <= PREP_END
        Tm = ctok[:, 0].rearrange("p (h n) -> p h n", h=8)
        Um = ctok[:, 1].rearrange("p (h n) -> p h n", h=8)
        Xs = brT[:].rearrange("p k t -> p (k t)")[:, 0:512]
        SAs = brT[:].rearrange("p k t -> p (k t)")[:, 512:1024]
        dif = eiL[:, 0:2]

        def pe_mix(pe, l):
            pe.wait_ge(rows_landed, pe.due(rows_landed, 16 * 9))
            pe.wait_ge(to_dve.freed, to_dve.next_free())
            bank = to_dve.free_bank()
            mm = pe.turn(bank[:, 0:P], rows[:])
            mm.then_inc(to_dve.filled, 1)
            pe.wait_ge(xT_ready, pe.due(xT_ready))
            blk = pe.block()
            pe_T(pe, blk, to_dve, 0, [P, P, 32])
            pe.used()
            for _ in range(3):
                blk = pe.block()
                pe_T(pe, blk, to_dve, 0, [P] * 4)
                pe.used()
            pe.wait_ge(lora_landed, pe.due(lora_landed, 16 * 5))
            pe.wait_ge(lora_in_ready, pe.due(lora_in_ready))
            for rows_ in (slice(0, 64), slice(64, 128)):
                for pair in range(2):
                    pe.wait_ge(to_act.freed, to_act.next_free())
                    bank = to_act.free_bank()
                    for j in range(2):
                        hp = 2 * pair + j
                        mm = pe.mm(bank[:, j * SEQ:(j + 1) * SEQ], lora_w[rows_, hp * P:(hp + 1) * P], loT[rows_, 0])
                        if j:
                            mm.then_inc(to_act.filled, 1)
            for tt in range(2):
                pe.wait_ge(to_act.freed, to_act.next_free())
                bank = to_act.free_bank()
                pe.mm(bank[:], loT[:, 1, tt * P:(tt + 1) * P], g2a, True, False)
                mm = pe.mm(bank[:], loT[0:32, 2, tt * P:(tt + 1) * P], g2b, False, True)
                mm.then_inc(to_act.filled, 1)
            blk = pe.block()
            pe_T(pe, blk, to_act, 0, [P] * 4)
            pe.used()
            pe.wait_ge(sq_ready, pe.due(sq_ready))
            for g in range(2):
                pe.wait_ge(to_dve.freed, to_dve.next_free())
                bank = to_dve.free_bank()
                mm = pe.mm(bank[:], half_ones, sq[:, 2 * g:2 * g + 2])
                mm.then_inc(to_dve.filled, 1)
            blk = pe.block()
            pe_tok(pe, blk, to_act, 0, 512, x_lhs)
            pe.used()
            blk = pe.block()
            pe_tok(pe, blk, to_act, 0, 512, x_lhs)
            pe.used()
            blk = pe.block(2)
            pe_T(pe, blk, to_act, 0, [16])
            pe_tok(pe, blk, to_act, 16, 8, x_lhs)
            pe.used()
            for _ in range(3):
                blk = pe.block()
                pe_T(pe, blk, to_act, 0, [P] * 4)
                pe.used()
            blk = pe.block()
            pe_tok(pe, blk, to_act, 0, 512, x_lhs)
            pe.used()
            pe.wait_ge(gla_in_ready, pe.due(gla_in_ready))
            pe.wait_ge(to_dve.freed, to_dve.next_free())
            bank = to_dve.free_bank()
            for hp in range(2):
                mm = pe.mm(bank[:, hp * SEQ:(hp + 1) * SEQ], gk2[:, hp * P:(hp + 1) * P], gla_lo[0:16, :])
                if hp:
                    mm.then_inc(to_dve.filled, 1)
            pe_gates(pe, 0)
            pe_gates(pe, 1)
            for mixer in (pe_rwkv, pe_gla, pe_gdn):
                mixer(pe)
                pe_branch(pe)
            pe_merged(pe)

        def pe_gates(pe, half):
            blk = pe.block()
            pe_tok(pe, blk, to_act, 0, 512, x_lhs)
            pe.used()

        def act_gate(act, half, tt):
            if half == tt == 0:
                if act.gates:
                    act.wait_ge(gates_used, act.due(gates_used))
                act.gates += 1
            act.wait_ge(to_act.filled, to_act.next_filled())
            bank = to_act.filled_bank()
            act.e.activation(gate_at(tt, half), bank[:].rearrange("p (a b) -> p a b", a=2),
                             ACT.Sigmoid).then_inc(to_act.freed, act.up(to_act.freed))
            act.wait_ge(to_act.freed, act.sent(to_act.freed))
            if half == tt == 1:
                act.sem_inc(gates_ready, act.up(gates_ready))

        def act_gates(act, half):
            for tt in range(2):
                act_gate(act, half, tt)

        def pe_branch(pe):
            for tt in range(2):
                pe.wait_ge(branch_ready, pe.due(branch_ready))
                pe.wait_ge(to_dve.freed, to_dve.next_free())
                bank = to_dve.free_bank()
                for k in range(4):
                    mm = pe.turn(bank[:, k * P:(k + 1) * P], br_tok[:, tt, k * P:(k + 1) * P])
                    if k == 3:
                        mm.then_inc(to_dve.filled, 1)
            pe.wait_ge(brT_ready, pe.due(brT_ready))
            blk = pe.block()
            wide4 = blk.rearrange("p k n -> p (k n)").rearrange("p (k n) -> p k n", n=D)
            for half in range(2):
                pe_tok(pe, wide4, to_dve, half * 512, 512, lambda k, tt: brT[:, k, tt * P:(tt + 1) * P], K=4)
            pe.used()

        def dve_branch(dve, n):
            v = nc.vector
            for tt in range(2):
                dve.wait_ge(to_dve.filled, to_dve.next_filled())
                bank = to_dve.filled_bank()
                ins = v.tensor_copy(brT[:, :, tt * P:(tt + 1) * P], bank[:].rearrange("p (k t) -> p k t", k=4))
                ins.then_inc(to_dve.freed, dve.up(to_dve.freed))
                dve.wait_ge(to_dve.freed, dve.sent(to_dve.freed))
            dve.sem_inc(brT_ready, dve.up(brT_ready))
            dve.wait_ge(gates_ready, dve.due(gates_ready))
            for half in range(2):
                for tt in range(2):
                    dve.wait_ge(to_dve.filled, to_dve.next_filled())
                    bank = to_dve.filled_bank()
                    g = gate_at(tt, half)
                    mg = merged[:, tt, half * 512:(half + 1) * 512]
                    b2 = bank[:].rearrange("p (a b) -> p a b", a=2)
                    if n == 0:
                        ins = v.tensor_tensor(mg.rearrange("p (a b) -> p a b", a=2), b2, g, ALU.mult)
                        ins.then_inc(to_dve.freed, dve.up(to_dve.freed))
                        dve.wait_ge(to_dve.freed, dve.sent(to_dve.freed))
                    else:
                        v.tensor_tensor(g, b2, g, ALU.mult).then_inc(to_dve.freed, dve.up(to_dve.freed))
                        dve.wait_ge(to_dve.freed, dve.sent(to_dve.freed))
                        ins = v.tensor_tensor(mg.rearrange("p (a b) -> p a b", a=2),
                                                     mg.rearrange("p (a b) -> p a b", a=2), g, ALU.add)
                        ins.then_inc(dve_step, dve.up(dve_step))
                        dve.wait_ge(dve_step, dve.sent(dve_step))
            dve.sem_inc(gates_used, dve.up(gates_used))

        def pe_merged(pe):
            for tt in range(2):
                pe.wait_ge(merged_ready, pe.due(merged_ready))
                for q in range(2):
                    pe.wait_ge(to_act.freed, to_act.next_free())
                    bank = to_act.free_bank()
                    for k in range(4):
                        kt = 4 * q + k
                        mm = pe.turn(bank[:, k * P:(k + 1) * P], merged[:, tt, kt * P:(kt + 1) * P])
                        if k == 3:
                            mm.then_inc(to_act.filled, 1)
            pe.wait_ge(xT_ready, pe.due(xT_ready))
            for half in range(2):
                blk = pe.block()
                pe_tok(pe, blk, to_dve, 0, 512, x_lhs)
                pe.used()

        def act_merged(act):
            for tt in range(2):
                for q in range(2):
                    act.wait_ge(to_act.filled, to_act.next_filled())
                    bank = to_act.filled_bank()
                    ins = act.e.copy(xT[:, 4 * q:4 * q + 4, tt * P:(tt + 1) * P],
                                                      bank[:].rearrange("p (k t) -> p k t", k=4))
                    ins.then_inc(to_act.freed, act.up(to_act.freed))
                    act.wait_ge(to_act.freed, act.sent(to_act.freed))
            act.sem_inc(xT_ready, act.up(xT_ready))

        def dve_mix(dve, l):
            v = nc.vector
            dve.wait_ge(to_dve.filled, to_dve.next_filled())
            bank = to_dve.filled_bank()
            v.tensor_copy(cols[:], bank[:, 0:P]).then_inc(to_dve.freed, dve.up(to_dve.freed))
            dve.wait_ge(to_dve.freed, dve.sent(to_dve.freed))
            dve.sem_inc(cols_free, dve.up(cols_free))
            ins = v.tensor_scalar(cols[:, OMKA:OMKA + 4], cols[:, KAR:KAR + 4], -1.0, 1.0, ALU.mult, ALU.add)
            ins.then_inc(cols_ready, dve.up(cols_ready))
            dve.wait_ge(cols_ready, dve.sent(cols_ready))
            dve.wait_ge(mix_rows_landed, dve.due(mix_rows_landed, 16 * 6))
            for n, mixer in enumerate((dve_rwkv, dve_gla, dve_gdn)):
                mixer(dve)
                dve_branch(dve, n)
            dve.sem_inc(merged_ready, dve.up(merged_ready))
            dve.sem_inc(merged_ready, dve.up(merged_ready))

        def act_mix(act, l):
            act_rwkv_inputs(act)
            act_rwkv_exps(act)
            for g in range(2):
                act.wait_ge(to_act.filled, to_act.next_filled())
                bank = to_act.filled_bank()
                ins = act.e.activation(gla_qk[:, 2 * g:2 * g + 2], bank[:].rearrange("p (a b) -> p a b", a=2),
                                                        ACT.Identity, scale=0.125 if g == 0 else 1.0)
                ins.then_inc(to_act.freed, act.up(to_act.freed))
                act.wait_ge(to_act.freed, act.sent(to_act.freed))
            act.wait_ge(ss_ready, act.due(ss_ready))
            act.e.activation(sq[:], sq[:], ACT.Sqrt).then_inc(norm_ready, act.up(norm_ready))
            act.wait_ge(norm_ready, act.sent(norm_ready))
            for tt in range(2):
                act.wait_ge(to_act.filled, to_act.next_filled())
                bank = to_act.filled_bank()
                act.e.copy(gla_v[:, tt], bank[:]).then_inc(to_act.freed, act.up(to_act.freed))
                act.wait_ge(to_act.freed, act.sent(to_act.freed))
            for tt in range(2):
                act.wait_ge(to_act.filled, to_act.next_filled())
                bank = to_act.filled_bank()
                act.e.activation(gla_gate[:, tt], bank[:], ACT.Silu).then_inc(to_act.freed, act.up(to_act.freed))
                act.wait_ge(to_act.freed, act.sent(to_act.freed))
            act.wait_ge(to_act.filled, to_act.next_filled())
            bank = to_act.filled_bank()
            act.e.copy(gla_lo[0:16, :], bank[0:16, 0:SEQ]).then_inc(to_act.freed, act.up(to_act.freed))
            act.wait_ge(to_act.freed, act.sent(to_act.freed))
            act.sem_inc(gla_in_ready, act.up(gla_in_ready))
            for tt in range(2):
                act.wait_ge(to_act.filled, to_act.next_filled())
                bank = to_act.filled_bank()
                act.e.copy(gdn_ab[:, tt], bank[:, 0:8]).then_inc(to_act.freed, act.up(to_act.freed))
                act.wait_ge(to_act.freed, act.sent(to_act.freed))
            for g in range(6):
                act.wait_ge(to_act.filled, to_act.next_filled())
                bank = to_act.filled_bank()
                ins = act.e.copy(gdn_T[:, 2 * g:2 * g + 2], bank[:].rearrange("p (a b) -> p a b", a=2))
                ins.then_inc(to_act.freed, act.up(to_act.freed))
                act.wait_ge(to_act.freed, act.sent(to_act.freed))
                act.sem_inc(gdn_T_ready, act.up(gdn_T_ready))
            for tt in range(2):
                act.wait_ge(to_act.filled, to_act.next_filled())
                bank = to_act.filled_bank()
                act.e.activation(gdn_gate[:, tt], bank[:], ACT.Silu).then_inc(to_act.freed, act.up(to_act.freed))
                act.wait_ge(to_act.freed, act.sent(to_act.freed))
            act.sem_inc(gdn_in_ready, act.up(gdn_in_ready))
            act_conv(act, range(12))
            act_gates(act, 0)
            act_gates(act, 1)
            for mixer in (act_rwkv, act_gla, act_gdn):
                mixer(act)
            act_merged(act)

        def act_rwkv_inputs(act):
            act.wait_ge(cols_ready, act.due(cols_ready))
            act.wait_ge(lora_mixed, act.due(lora_mixed))
            act.e.activation(loT[0:64, 0], loT[0:64, 0], ACT.Tanh).then_inc(act_step, act.up(act_step))
            act.wait_ge(act_step, act.sent(act_step))
            act.e.activation(loT[:, 1], loT[:, 1], ACT.Sigmoid).then_inc(act_step, act.up(act_step))
            act.wait_ge(act_step, act.sent(act_step))
            act.e.activation(loT[0:32, 2], loT[0:32, 2], ACT.Sigmoid).then_inc(lora_in_ready, act.up(lora_in_ready))
            act.wait_ge(lora_in_ready, act.sent(lora_in_ready))
            for dst, col, ready in ((sw, W0, sw_ready), (bT, A0, a_ready)):
                for pair in range(2):
                    act.wait_ge(to_act.filled, to_act.next_filled())
                    bank = to_act.filled_bank()
                    for j in range(2):
                        hp = 2 * pair + j
                        ins = act.e.activation(dst[:, hp], bank[:, j * SEQ:(j + 1) * SEQ], ACT.Sigmoid,
                                               bias=cols[:, col + hp:col + hp + 1])
                        if j:
                            ins.then_inc(to_act.freed, act.up(to_act.freed))
                            act.wait_ge(to_act.freed, act.sent(to_act.freed))
                        else:
                            ins.then_inc(act_step, act.up(act_step))
                            act.wait_ge(act_step, act.sent(act_step))
                act.sem_inc(ready, act.up(ready))
            for tt in range(2):
                act.wait_ge(to_act.filled, to_act.next_filled())
                bank = to_act.filled_bank()
                act.e.copy(g_tok[:, tt], bank[:]).then_inc(to_act.freed, act.up(to_act.freed))
                act.wait_ge(to_act.freed, act.sent(to_act.freed))
            act.sem_inc(g_ready, act.up(g_ready))

        def act_rwkv_exps(act):
            act.wait_ge(L_ready, act.due(L_ready))
            act.e.activation(eiL[:], eL[:], ACT.Exp, scale=RWK_C).then_inc(act_step, act.up(act_step))
            act.wait_ge(act_step, act.sent(act_step))
            act.e.activation(eL[:], eL[:], ACT.Exp, scale=-RWK_C).then_inc(act_step, act.up(act_step))
            act.wait_ge(act_step, act.sent(act_step))
            act.e.activation(eLx[:], eLx[:], ACT.Exp, scale=-RWK_C).then_inc(expL_ready, act.up(expL_ready))
            act.wait_ge(expL_ready, act.sent(expL_ready))

        def act_rwkv(act):
            for tt in range(2):
                act_solve(act, Am)
                act_head_std(act)

        def act_head_std(act):
            act.wait_ge(head_var_ready, act.due(head_var_ready))
            ins = act.e.activation(small[:, 24:32], small[:, 16:24], ACT.Sqrt)
            ins.then_inc(head_std_ready, act.up(head_std_ready))
            act.wait_ge(head_std_ready, act.sent(head_std_ready))

        def dve_rwkv(dve):
            v = nc.vector
            for dst, r0 in ((AR[:, 0:1], 64), (AR[:, 1:2], 0), (AR[:, 2:3], 64), (AR[:, 3:4], 0)):
                v.memset(dst[r0:r0 + 64], 0.0).then_inc(dve_step, dve.up(dve_step))
                dve.wait_ge(dve_step, dve.sent(dve_step))
            tiles = [(loT, 0, 12, P), (loT, 1, 13, P), (loT, 2, 14, 32)]
            for dst, t0 in ((r_T, 0), (k_T, 4), (vT, 8)):
                tiles += [(dst, j, t0 + j, P) for j in range(4)]
            groups = [tiles[0:2], tiles[2:3]] + [tiles[i:i + 2] for i in range(3, 15, 2)]
            for gi, group in enumerate(groups):
                dve.wait_ge(to_dve.filled, to_dve.next_filled())
                bank = to_dve.filled_bank()
                n = group[0][3]
                b3 = bank[0:n, 0:len(group) * SEQ].rearrange("p (a t) -> p a t", a=len(group))
                d3 = dif[0:n, 0:len(group)]
                v.tensor_copy(d3, b3).then_inc(dve_step, dve.up(dve_step))
                dve.wait_ge(dve_step, dve.sent(dve_step))
                v.tensor_tensor(sq[0:n, 0:len(group), 1:SEQ], d3[:, :, 0:SEQ - 1], d3[:, :, 1:SEQ],
                                       ALU.subtract).then_inc(dve_step, dve.up(dve_step))
                dve.wait_ge(dve_step, dve.sent(dve_step))
                ins = v.tensor_scalar(sq[0:n, 0:len(group), 0:1], d3[:, :, 0:1], -1.0, None, ALU.mult)
                ins.then_inc(dve_step, dve.up(dve_step))
                dve.wait_ge(dve_step, dve.sent(dve_step))
                for j, (dst, k, t, _) in enumerate(group):
                    ins = v.scalar_tensor_tensor(out=dst[0:n, k], in0=sq[0:n, j], scalar=cols[0:n, MU + t:MU + t + 1],
                                                 in1=b3[:, j], op0=ALU.mult, op1=ALU.add)
                    if j == len(group) - 1:
                        ins.then_inc(to_dve.freed, dve.up(to_dve.freed))
                        dve.wait_ge(to_dve.freed, dve.sent(to_dve.freed))
                    else:
                        ins.then_inc(dve_step, dve.up(dve_step))
                        dve.wait_ge(dve_step, dve.sent(dve_step))
                if gi == 1:
                    dve.sem_inc(lora_mixed, dve.up(lora_mixed))
            dve.wait_ge(sw_ready, dve.due(sw_ready))
            for hp in range(4):
                ins = v.tensor_tensor_scan(eL[:, hp], resets, sw[:, hp], 0.0, ALU.mult, ALU.add)
                ins.then_inc(dve_step, dve.up(dve_step))
                dve.wait_ge(dve_step, dve.sent(dve_step))
            v.tensor_tensor(eLx[:], eL[:], sw[:], ALU.subtract).then_inc(L_ready, dve.up(L_ready))
            dve.wait_ge(L_ready, dve.sent(L_ready))
            for hp in range(4):
                ins = v.tensor_scalar(sw[:, hp], k_T[:, hp], cols[:, KKR + hp:KKR + hp + 1], None, ALU.mult)
                ins.then_inc(dve_step, dve.up(dve_step))
                dve.wait_ge(dve_step, dve.sent(dve_step))
            v.tensor_tensor(sq[:], sw[:], sw[:], ALU.mult).then_inc(sq_ready, dve.up(sq_ready))
            dve.wait_ge(sq_ready, dve.sent(sq_ready))
            for g in range(2):
                dve.wait_ge(to_dve.filled, to_dve.next_filled())
                bank = to_dve.filled_bank()
                v.tensor_scalar(sq[:, 2 * g:2 * g + 2], bank[:].rearrange("p (a t) -> p a t", a=2),
                                                 1e-6, None, ALU.add).then_inc(to_dve.freed, dve.up(to_dve.freed))
                dve.wait_ge(to_dve.freed, dve.sent(to_dve.freed))
            dve.sem_inc(ss_ready, dve.up(ss_ready))
            dve.wait_ge(norm_ready, dve.due(norm_ready))
            v.reciprocal(sq[:], sq[:]).then_inc(dve_step, dve.up(dve_step))
            dve.wait_ge(dve_step, dve.sent(dve_step))
            v.tensor_tensor(sw[:], sw[:], sq[:], ALU.mult).then_inc(dve_step, dve.up(dve_step))
            dve.wait_ge(dve_step, dve.sent(dve_step))
            dve.wait_ge(a_ready, dve.due(a_ready))
            for hp in range(4):
                ins = v.tensor_scalar(sq[:, hp], bT[:, hp], cols[:, KAR + hp:KAR + hp + 1],
                                             cols[:, OMKA + hp:OMKA + hp + 1], ALU.mult, ALU.add)
                ins.then_inc(dve_step, dve.up(dve_step))
                dve.wait_ge(dve_step, dve.sent(dve_step))
            v.tensor_tensor(k_T[:], k_T[:], sq[:], ALU.mult).then_inc(dve_step, dve.up(dve_step))
            dve.wait_ge(dve_step, dve.sent(dve_step))
            v.tensor_tensor(bT[:], bT[:], sw[:], ALU.mult).then_inc(dve_step, dve.up(dve_step))
            dve.wait_ge(dve_step, dve.sent(dve_step))
            for hp in range(4):
                ins = v.scalar_tensor_tensor(out=sq[:, hp], in0=r_T[:, hp], scalar=cols[:, RKR + hp:RKR + hp + 1],
                                                    in1=k_T[:, hp], op0=ALU.mult, op1=ALU.mult)
                ins.then_inc(dve_step, dve.up(dve_step))
                dve.wait_ge(dve_step, dve.sent(dve_step))
            dve.sem_inc(bonus_in_ready, dve.up(bonus_in_ready))
            dve.wait_ge(expL_ready, dve.due(expL_ready))
            for par in range(2):
                r_ = slice(64 * par, 64 * par + 64)
                v.scalar_tensor_tensor(out=AR[r_, par], in0=sw[r_], scalar=-1.0, in1=eLx[r_],
                                              op0=ALU.mult, op1=ALU.mult).then_inc(dve_step, dve.up(dve_step))
                dve.wait_ge(dve_step, dve.sent(dve_step))
                v.tensor_tensor(AR[r_, 2 + par], r_T[r_], eL[r_], ALU.mult).then_inc(dve_step, dve.up(dve_step))
                dve.wait_ge(dve_step, dve.sent(dve_step))
            v.tensor_tensor(k_T[:], k_T[:], eiL[:], ALU.mult).then_inc(dve_step, dve.up(dve_step))
            dve.wait_ge(dve_step, dve.sent(dve_step))
            v.tensor_tensor(bT[:], bT[:], eiL[:], ALU.mult).then_inc(rwkv_T_ready, dve.up(rwkv_T_ready))
            dve.wait_ge(rwkv_T_ready, dve.sent(rwkv_T_ready))
            dve.wait_ge(to_dve.filled, to_dve.next_filled())
            bank = to_dve.filled_bank()
            ins = v.tensor_copy(gla_z[:], bank[:].rearrange("p (a t) -> p a t", a=2))
            ins.then_inc(to_dve.freed, dve.up(to_dve.freed))
            dve.wait_ge(to_dve.freed, dve.sent(to_dve.freed))
            dve.sem_inc(lora_used, dve.up(lora_used))
            dve_conv(dve)
            dve.wait_ge(to_dve.filled, to_dve.next_filled())
            bank = to_dve.filled_bank()
            v.tensor_copy(bonus, bank[:, 0:16]).then_inc(to_dve.freed, dve.up(to_dve.freed))
            dve.wait_ge(to_dve.freed, dve.sent(to_dve.freed))
            for tt in range(2):
                dve.wait_ge(to_dve.filled, to_dve.next_filled())
                bank = to_dve.filled_bank()
                v.tensor_copy(v_tok[:, tt], bank[:]).then_inc(to_dve.freed, dve.up(to_dve.freed))
                dve.wait_ge(to_dve.freed, dve.sent(to_dve.freed))
            v.memset(Hst[:], 0.0).then_inc(dve_step, dve.up(dve_step))
            dve.wait_ge(dve_step, dve.sent(dve_step))
            v.memset(Xs, 0.0).then_inc(dve_step, dve.up(dve_step))
            dve.wait_ge(dve_step, dve.sent(dve_step))
            v.memset(SAs, 0.0).then_inc(dve_step, dve.up(dve_step))
            dve.wait_ge(dve_step, dve.sent(dve_step))
            dve.sem_inc(v_tok_ready, dve.up(v_tok_ready))
            dve.sem_inc(state_ready, dve.up(state_ready))
            dve.wait_ge(g_ready, dve.due(g_ready))
            for tt in range(2):
                for j in range(2):
                    dve.wait_ge(to_dve.filled, to_dve.next_filled())
                    bank = to_dve.filled_bank()
                    v.tensor_copy(BKtok[:, j], bank[:]).then_inc(to_dve.freed, dve.up(to_dve.freed))
                    dve.wait_ge(to_dve.freed, dve.sent(to_dve.freed))
                dve.sem_inc(bk_tok_ready, dve.up(bk_tok_ready))
                for h in range(8):
                    dve.wait_ge(to_dve.filled, to_dve.next_filled())
                    bank = to_dve.filled_bank()
                    ins = (v.tensor_tensor(
                              M4[:, h].rearrange("p (x a) n -> p x (a n)", x=2), bank[:].rearrange("p (x n) -> p x n", x=2),
                              causal2.unsqueeze(1).broadcast_to([P, 2, 2 * P]), ALU.mult))
                    ins.then_inc(to_dve.freed, dve.up(to_dve.freed))
                    dve.wait_ge(to_dve.freed, dve.sent(to_dve.freed))
                for b in range(2):
                    dve_solve_start(dve, Um[:, 4 * b:4 * b + 4], M4[:, 4 * b:4 * b + 4, 2])
                dve_solve(dve, lambda b: M4[:, 4 * b:4 * b + 4, 2], Tm, Um, Am)
                for c in range(2):
                    r_ = slice(64 * c, 64 * c + 64)
                    dve.wait_ge(to_dve.filled, to_dve.next_filled())
                    bank = to_dve.filled_bank()
                    v.tensor_copy(Xs[r_], bank[r_, :]).then_inc(to_dve.freed, dve.up(to_dve.freed))
                    dve.wait_ge(to_dve.freed, dve.sent(to_dve.freed))
                    dve.sem_inc(x_rows_ready, dve.up(x_rows_ready))
                    dve.wait_ge(to_dve.filled, to_dve.next_filled())
                    bank = to_dve.filled_bank()
                    v.tensor_copy(SAs[r_], bank[r_, :]).then_inc(to_dve.freed, dve.up(to_dve.freed))
                    dve.wait_ge(to_dve.freed, dve.sent(to_dve.freed))
                    dve.sem_inc(sa_ready, dve.up(sa_ready))
                    dve.wait_ge(to_dve.filled, to_dve.next_filled())
                    bank = to_dve.filled_bank()
                    v.tensor_copy(br_tok[r_, tt], bank[r_, :]).then_inc(to_dve.freed, dve.up(to_dve.freed))
                    dve.wait_ge(to_dve.freed, dve.sent(to_dve.freed))
                    dve.wait_ge(to_dve.filled, to_dve.next_filled())
                    bank = to_dve.filled_bank()
                    v.tensor_tensor(Hst[:], bank[:, 0:256].rearrange("p (a n) -> p a n", a=4), Hst[:],
                                                     ALU.add).then_inc(to_dve.freed, dve.up(to_dve.freed))
                    dve.wait_ge(to_dve.freed, dve.sent(to_dve.freed))
                    e = P * tt + 64 * c + 63
                    ins = v.tensor_tensor(Hst[:], Hst[:], eL[:, :, e:e + 1].broadcast_to([P, 4, 64]), ALU.mult)
                    ins.then_inc(state_ready, dve.up(state_ready))
                    dve.wait_ge(state_ready, dve.sent(state_ready))
                y = br_tok[:, tt]
                y3 = y.rearrange("p (h n) -> p h n", h=8)
                t3 = gn_tmp.rearrange("p (h n) -> p h n", h=8)
                v.tensor_reduce(small[:, 8:16], y3, AX.X, ALU.add).then_inc(dve_step, dve.up(dve_step))
                dve.wait_ge(dve_step, dve.sent(dve_step))
                ins = v.tensor_scalar(small[:, 8:16], small[:, 8:16], 1.0 / 64, None, ALU.mult)
                ins.then_inc(dve_step, dve.up(dve_step))
                dve.wait_ge(dve_step, dve.sent(dve_step))
                ins = v.tensor_tensor(y3, y3, small[:, 8:16].unsqueeze(2).broadcast_to([P, 8, 64]), ALU.subtract)
                ins.then_inc(dve_step, dve.up(dve_step))
                dve.wait_ge(dve_step, dve.sent(dve_step))
                dve_head_std(dve, y3, t3, 8, 64, 64e-5)
                v.tensor_tensor(y, y, gnp[:, 0], ALU.mult).then_inc(dve_step, dve.up(dve_step))
                dve.wait_ge(dve_step, dve.sent(dve_step))
                v.tensor_tensor(y, y, gnp[:, 1], ALU.add).then_inc(dve_step, dve.up(dve_step))
                dve.wait_ge(dve_step, dve.sent(dve_step))
                ins = (v.tensor_tensor(t3, v_tok[:, tt].rearrange("p (h n) -> p h n", h=8),
                                             bonus[:, 8 * tt:8 * tt + 8].unsqueeze(2).broadcast_to([P, 8, 64]), ALU.mult))
                ins.then_inc(dve_step, dve.up(dve_step))
                dve.wait_ge(dve_step, dve.sent(dve_step))
                v.tensor_tensor(y, y, gn_tmp, ALU.add).then_inc(dve_step, dve.up(dve_step))
                dve.wait_ge(dve_step, dve.sent(dve_step))
                v.tensor_tensor(y, y, g_tok[:, tt], ALU.mult).then_inc(branch_ready, dve.up(branch_ready))
                dve.wait_ge(branch_ready, dve.sent(branch_ready))

        def dve_head_std(dve, y3, t3, heads, n, eps):
            v = nc.vector
            v.tensor_tensor(t3, y3, y3, ALU.mult).then_inc(dve_step, dve.up(dve_step))
            dve.wait_ge(dve_step, dve.sent(dve_step))
            v.tensor_reduce(small[:, 16:16 + heads], t3, AX.X, ALU.add).then_inc(dve_step, dve.up(dve_step))
            dve.wait_ge(dve_step, dve.sent(dve_step))
            if heads < 8:
                v.memset(small[:, 16 + heads:24], 0.0).then_inc(dve_step, dve.up(dve_step))
                dve.wait_ge(dve_step, dve.sent(dve_step))
            ins = v.tensor_scalar(small[:, 16:24], small[:, 16:24], 1.0 / n, eps, ALU.mult, ALU.add)
            ins.then_inc(head_var_ready, dve.up(head_var_ready))
            dve.wait_ge(head_var_ready, dve.sent(head_var_ready))
            dve.wait_ge(head_std_ready, dve.due(head_std_ready))
            v.reciprocal(small[:, 24:32], small[:, 24:32]).then_inc(dve_step, dve.up(dve_step))
            dve.wait_ge(dve_step, dve.sent(dve_step))
            ins = v.tensor_tensor(y3, y3, small[:, 24:24 + heads].unsqueeze(2).broadcast_to([P, heads, n]), ALU.mult)
            ins.then_inc(dve_step, dve.up(dve_step))
            dve.wait_ge(dve_step, dve.sent(dve_step))

        def dve_solve_start(dve, U, AT):
            v = nc.vector
            ins = v.tensor_tensor(U, AT, lvlT[:, 0:1].broadcast_to([P, 4, P]), ALU.mult)
            ins.then_inc(dve_step, dve.up(dve_step))
            dve.wait_ge(dve_step, dve.sent(dve_step))
            ins = v.tensor_tensor(U, U, ident.unsqueeze(1).broadcast_to([P, 4, P]), ALU.add)
            ins.then_inc(solve_started, dve.up(solve_started))
            dve.wait_ge(solve_started, dve.sent(solve_started))

        def dve_solve(dve, AT, Tm, Um, Am):
            v = nc.vector
            for b in range(2):
                dve.wait_ge(to_dve.filled, to_dve.next_filled())
                bank = to_dve.filled_bank()
                ins = v.tensor_copy(Tm[:, 4 * b:4 * b + 4], bank[:].rearrange("p (h n) -> p h n", h=4))
                ins.then_inc(to_dve.freed, dve.up(to_dve.freed))
                dve.wait_ge(to_dve.freed, dve.sent(to_dve.freed))

            def mask(l, b):
                v.tensor_tensor(Am[:, 4 * b:4 * b + 4], AT(b), lvlT[:, l:l + 1].broadcast_to([P, 4, P]),
                                ALU.mult).then_inc(level_masked, dve.up(level_masked))

            for b in range(2):
                mask(1, b)
            for l in range(1, len(LEVELS)):
                for b in range(2):
                    for M in ((Tm, Um) if l < len(LEVELS) - 1 else (Um,)):
                        dve.wait_ge(to_dve.filled, to_dve.next_filled())
                        bank = to_dve.filled_bank()
                        X = M[:, 4 * b:4 * b + 4]
                        ins = v.tensor_tensor(X, bank[:].rearrange("p (h n) -> p h n", h=4), X, ALU.add)
                        ins.then_inc(to_dve.freed, dve.up(to_dve.freed))
                    if l < len(LEVELS) - 1:
                        mask(l + 1, b)
                dve.wait_ge(to_dve.freed, dve.sent(to_dve.freed))
            dve.sem_inc(solved, dve.up(solved))

        def act_solve(act, Am):
            for l in range(1, len(LEVELS)):
                for b in range(2):
                    act.wait_ge(to_act.filled, to_act.next_filled())
                    bank = to_act.filled_bank()
                    ins = act.e.copy(Am[:, 4 * b:4 * b + 4], bank[:].rearrange("p (h n) -> p h n", h=4))
                    ins.then_inc(to_act.freed, act.up(to_act.freed))
                    act.wait_ge(to_act.freed, act.sent(to_act.freed))
                    act.sem_inc(level_product_ready, act.up(level_product_ready))

        def pe_solve(pe, Tm, Um, Am):
            for b in range(2):
                pe.wait_ge(solve_started, pe.due(solve_started))
                pe.wait_ge(to_dve.freed, to_dve.next_free())
                bank = to_dve.free_bank()
                for h in range(4):
                    mm = pe.turn(bank[:, h * P:(h + 1) * P], Um[:, 4 * b + h])
                    if h == 3:
                        mm.then_inc(to_dve.filled, 1)
            for l in range(1, len(LEVELS)):
                for b in range(2):
                    pe.wait_ge(level_masked, pe.due(level_masked))
                    pe.wait_ge(to_act.freed, to_act.next_free())
                    bank = to_act.free_bank()
                    for h in range(4):
                        mm = pe.mm(bank[:, h * P:(h + 1) * P], Am[:, 4 * b + h], Tm[:, 4 * b + h])
                        if h == 3:
                            mm.then_inc(to_act.filled, 1)
                for b in range(2):
                    pe.wait_ge(level_product_ready, pe.due(level_product_ready))
                    if l < len(LEVELS) - 1:
                        pe.wait_ge(to_dve.freed, to_dve.next_free())
                        bank = to_dve.free_bank()
                        for h in range(4):
                            mm = pe.mm(bank[:, h * P:(h + 1) * P], Um[:, 4 * b + h], Am[:, 4 * b + h])
                            if h == 3:
                                mm.then_inc(to_dve.filled, 1)
                    pe.wait_ge(to_dve.freed, to_dve.next_free())
                    bank = to_dve.free_bank()
                    for h in range(4):
                        mm = pe.mm(bank[:, h * P:(h + 1) * P], Am[:, 4 * b + h], Um[:, 4 * b + h])
                        if h == 3:
                            mm.then_inc(to_dve.filled, 1)
            pe.wait_ge(solved, pe.due(solved))

        def pe_rwkv(pe):
            pe.wait_ge(bonus_in_ready, pe.due(bonus_in_ready))
            pe.wait_ge(to_dve.freed, to_dve.next_free())
            bank = to_dve.free_bank()
            for tt in range(2):
                for hp in range(4):
                    o = 8 * tt + 2 * hp
                    mm = pe.mm(bank[:, o:o + 2], sq[:, hp, tt * P:(tt + 1) * P], head_sel)
                    if tt and hp == 3:
                        mm.then_inc(to_dve.filled, 1)
            for tt in range(2):
                pe.wait_ge(to_dve.freed, to_dve.next_free())
                bank = to_dve.free_bank()
                for hp in range(4):
                    mm = pe.turn(bank[:, hp * P:(hp + 1) * P], vT[:, hp, tt * P:(tt + 1) * P])
                    if hp == 3:
                        mm.then_inc(to_dve.filled, 1)
            pe.wait_ge(rwkv_T_ready, pe.due(rwkv_T_ready))
            pe.wait_ge(v_tok_ready, pe.due(v_tok_ready))
            for tt in range(2):
                toks = slice(tt * P, (tt + 1) * P)
                for src in (bT, k_T):
                    pe.wait_ge(to_dve.freed, to_dve.next_free())
                    bank = to_dve.free_bank()
                    for hp in range(4):
                        mm = pe.turn(bank[:, hp * P:(hp + 1) * P], src[:, hp, toks])
                        if hp == 3:
                            mm.then_inc(to_dve.filled, 1)
                for h in range(8):
                    hp, par = h // 2, h % 2
                    pe.wait_ge(to_dve.freed, to_dve.next_free())
                    bank = to_dve.free_bank()
                    ar = AR[:, par::2, hp, toks]
                    pe.mm(bank[:, 0:256], k_T[:, hp, toks], ar)
                    mm = pe.mm(bank[:, 256:512], bT[:, hp, toks], ar)
                    mm.then_inc(to_dve.filled, 1)
                pe.wait_ge(bk_tok_ready, pe.due(bk_tok_ready))
                pe_solve(pe, Tm, Um, Am)
                for c in range(2):
                    r_ = slice(64 * c, 64 * c + 64)
                    ct = slice(tt * P + 64 * c, tt * P + 64 * c + 64)
                    pe.wait_ge(state_ready, pe.due(state_ready))
                    pe.wait_ge(to_dve.freed, to_dve.next_free())
                    bank = to_dve.free_bank()
                    for h in range(8):
                        hp, par = h // 2, h % 2
                        o = bank[r_, h * 64:(h + 1) * 64]
                        pe.mm(o, AR[:, par, hp, ct], Hst[:, hp], True, False)
                        mm = pe.mm(o, M4[:, h, 0, r_], v_tok[:, tt, h * 64:(h + 1) * 64], False, True)
                        if h == 7:
                            mm.then_inc(to_dve.filled, 1)
                    pe.wait_ge(x_rows_ready, pe.due(x_rows_ready))
                    pe.wait_ge(to_dve.freed, to_dve.next_free())
                    bank = to_dve.free_bank()
                    for h in range(8):
                        mm = pe.mm(bank[r_, h * 64:(h + 1) * 64], Um[:, h, r_], Xs[:, h * 64:(h + 1) * 64])
                        if h == 7:
                            mm.then_inc(to_dve.filled, 1)
                    pe.wait_ge(sa_ready, pe.due(sa_ready))
                    pe.wait_ge(to_dve.freed, to_dve.next_free())
                    bank = to_dve.free_bank()
                    for h in range(8):
                        hp, par = h // 2, h % 2
                        o = bank[r_, h * 64:(h + 1) * 64]
                        pe.mm(o, AR[:, 2 + par, hp, ct], Hst[:, hp], True, False)
                        pe.mm(o, M4[:, h, 1, r_], v_tok[:, tt, h * 64:(h + 1) * 64], False, False)
                        mm = pe.mm(o, M4[:, h, 3, r_], SAs[:, h * 64:(h + 1) * 64], False, True)
                        if h == 7:
                            mm.then_inc(to_dve.filled, 1)
                    pe.wait_ge(to_dve.freed, to_dve.next_free())
                    bank = to_dve.free_bank()
                    for h in range(8):
                        hp, par = h // 2, h % 2
                        o = bank[64 * par:64 * par + 64, hp * 64:(hp + 1) * 64]
                        pe.mm(o, BKtok[r_, 0, h * 64:(h + 1) * 64], SAs[r_, h * 64:(h + 1) * 64], True, False)
                        mm = pe.mm(o, BKtok[r_, 1, h * 64:(h + 1) * 64],
                                   v_tok[r_, tt, h * 64:(h + 1) * 64], False, True)
                        if h == 7:
                            mm.then_inc(to_dve.filled, 1)
            pe.wait_ge(state_ready, pe.due(state_ready))

        def halves(x, h, forward):
            v3 = x.rearrange("p (n t) -> p n t", t=2 * h)
            right, left = v3[:, :, h:2 * h], v3[:, :, 0:h]
            return (right, left) if forward else (left, right)

        def act_levels(act, F, scale, forward=True, late_unit=None):
            for l, h in enumerate(LEVELS):
                fq, fk = halves(F, h, forward)
                act.wait_ge(diff_ready, act.due(diff_ready))
                act.e.activation(fq, fq, ACT.Exp, scale=scale).then_inc(act_step, act.up(act_step))
                act.wait_ge(act_step, act.sent(act_step))
                act.e.activation(fk, fk, ACT.Exp, scale=-scale).then_inc(decay_ready, act.up(decay_ready))
                act.wait_ge(decay_ready, act.sent(decay_ready))
                if late_unit:
                    late_unit(l)

        def dve_levels(dve, b, q, k, F, write_q, kF, att, forward=True):
            v = nc.vector
            for bank_att in att:
                v.memset(bank_att, 0.0).then_inc(dve_step, dve.up(dve_step))
                dve.wait_ge(dve_step, dve.sent(dve_step))

            def diff(h):
                n = b.shape[1] // (2 * h)
                b3 = b.rearrange("p (n t) -> p n t", t=2 * h)
                border = b3[:, :, h - 1:h] if forward else b3[:, :, h:h + 1]
                ins = v.tensor_tensor(F.rearrange("p (n t) -> p n t", t=2 * h), b3,
                                      border.broadcast_to([P, n, 2 * h]), ALU.subtract)
                ins.then_inc(diff_ready, dve.up(diff_ready))
                dve.wait_ge(diff_ready, dve.sent(diff_ready))

            for l, h in [(None, None)] + list(enumerate(LEVELS)):
                if h is None:
                    write_q(None, None)
                    v.tensor_copy(kF, k).then_inc(level_ready, dve.up(level_ready))
                    dve.wait_ge(level_ready, dve.sent(level_ready))
                    mask = ident.unsqueeze(1)
                else:
                    dve.wait_ge(decay_ready, dve.due(decay_ready))
                    write_q(h, F)
                    ins = v.tensor_tensor(halves(kF, h, forward)[1], halves(k, h, forward)[1],
                                                 halves(F, h, forward)[1], ALU.mult)
                    ins.then_inc(level_ready, dve.up(level_ready))
                    dve.wait_ge(level_ready, dve.sent(level_ready))
                    mask = (lvlT if forward else lvl)[:, l:l + 1]
                if h != LEVELS[-1]:
                    diff(LEVELS[0] if h is None else LEVELS[l + 1])
                for bank_att in att:
                    dve.wait_ge(to_dve.filled, to_dve.next_filled())
                    bank = to_dve.filled_bank()
                    ins = v.copy_predicated(bank_att, mask.bitcast(U32).broadcast_to([P, 4, P]),
                                                             bank[:].rearrange("p (h n) -> p h n", h=4))
                    ins.then_inc(to_dve.freed, dve.up(to_dve.freed))
                dve.wait_ge(to_dve.freed, dve.sent(to_dve.freed))

        def pe_levels(pe, kF_at, Q_at, batches, late_unit=None):
            for l in range(1 + len(LEVELS)):
                if late_unit:
                    late_unit(l)
                pe.wait_ge(level_ready, pe.due(level_ready))
                for batch in batches:
                    pe.wait_ge(to_dve.freed, to_dve.next_free())
                    bank = to_dve.free_bank()
                    for j, (h, tt) in enumerate(batch):
                        mm = pe.mm(bank[:, j * P:(j + 1) * P], kF_at(h, tt), Q_at(h, tt))
                        if j == 3:
                            mm.then_inc(to_dve.filled, 1)

        g = Bump(WORK)
        gb = g(512)
        gE = g(512)
        gF = g(512)
        gtmp = g(512)
        gkend = g(512)
        gkF = g(512)
        gQ = g(2, 512)
        gQb = g(2, 512)
        gatt = g(2, 4, P)
        gktok = g(2, 256)
        gS = g(2, P)
        gtmp2 = g(512)

        def act_gla(act):
            act.wait_ge(gk_abs_ready, act.due(gk_abs_ready))
            act.e.activation(gtmp, gtmp, ACT.Exp, scale=-1.0).then_inc(act_step, act.up(act_step))
            act.wait_ge(act_step, act.sent(act_step))
            act.e.activation(gtmp, gtmp, ACT.Ln, bias=1.0).then_inc(gk_log_ready, act.up(gk_log_ready))
            act.wait_ge(gk_log_ready, act.sent(gk_log_ready))
            act.wait_ge(gb_ready, act.due(gb_ready))
            act.e.activation(gE, gb, ACT.Exp, scale=1.0 / 16).then_inc(act_step, act.up(act_step))
            act.wait_ge(act_step, act.sent(act_step))
            act.e.activation(gkend, gkend, ACT.Exp, scale=1.0 / 16).then_inc(gE_ready, act.up(gE_ready))
            act.wait_ge(gE_ready, act.sent(gE_ready))
            act_gates(act, 0)

            def late_unit(l):
                if l in (1, 3):
                    act_gate(act, 1, l // 2)

            act_levels(act, gF, 1.0 / 16, True, late_unit)
            for _ in range(2):
                act_head_std(act)

        def dve_gla(dve):
            v = nc.vector
            dve.wait_ge(gla_in_ready, dve.due(gla_in_ready))
            q = gla_qk[:, 0:2].rearrange("p a t -> p (a t)")
            k = gla_qk[:, 2:4].rearrange("p a t -> p (a t)")
            z = gla_z[:].rearrange("p a t -> p (a t)")
            for hp in range(2):
                ins = v.tensor_scalar(gla_z[:, hp], gla_z[:, hp], cols[:, GKB + hp:GKB + hp + 1], None, ALU.add)
                ins.then_inc(dve_step, dve.up(dve_step))
                dve.wait_ge(dve_step, dve.sent(dve_step))
            ins = v.scalar_tensor_tensor(out=gtmp, in0=z, scalar=-1.0, in1=z, op0=ALU.mult, op1=ALU.max)
            ins.then_inc(gk_abs_ready, dve.up(gk_abs_ready))
            dve.wait_ge(gk_abs_ready, dve.sent(gk_abs_ready))
            v.memset(gQ[:], 0.0).then_inc(dve_step, dve.up(dve_step))
            dve.wait_ge(dve_step, dve.sent(dve_step))
            v.memset(gQb[:], 0.0).then_inc(dve_step, dve.up(dve_step))
            dve.wait_ge(dve_step, dve.sent(dve_step))
            v.memset(gS[:], 0.0).then_inc(dve_step, dve.up(dve_step))
            dve.wait_ge(dve_step, dve.sent(dve_step))
            dve.wait_ge(gk_log_ready, dve.due(gk_log_ready))
            ins = v.scalar_tensor_tensor(out=gtmp2, in0=z, scalar=0.0, in1=gtmp, op0=ALU.min, op1=ALU.subtract)
            ins.then_inc(dve_step, dve.up(dve_step))
            dve.wait_ge(dve_step, dve.sent(dve_step))
            for hp in range(2):
                s_ = slice(hp * SEQ, (hp + 1) * SEQ)
                ins = v.tensor_tensor_scan(gb[:, s_], resets, gtmp2[:, s_], 0.0, ALU.mult, ALU.add)
                ins.then_inc(dve_step, dve.up(dve_step))
                dve.wait_ge(dve_step, dve.sent(dve_step))
            b3 = gb.rearrange("p (n t) -> p n t", t=C)
            v.tensor_tensor(gkend.rearrange("p (n t) -> p n t", t=C), b3[:, :, C - 1:C].broadcast_to([P, 8, C]),
                                   b3, ALU.subtract).then_inc(gb_ready, dve.up(gb_ready))
            dve.wait_ge(gb_ready, dve.sent(gb_ready))
            dve.wait_ge(gE_ready, dve.due(gE_ready))
            for par in range(2):
                r_ = slice(64 * par, 64 * par + 64)
                v.tensor_tensor(gQb[r_, par], q[r_], gE[r_], ALU.mult).then_inc(dve_step, dve.up(dve_step))
                dve.wait_ge(dve_step, dve.sent(dve_step))
            v.tensor_tensor(gkend, gkend, k, ALU.mult).then_inc(kend_ready, dve.up(kend_ready))
            dve.wait_ge(kend_ready, dve.sent(kend_ready))
            dve.wait_ge(to_dve.filled, to_dve.next_filled())
            bank = to_dve.filled_bank()
            ins = v.tensor_copy(gktok[:].rearrange("p t n -> p (t n)"), bank[:])
            ins.then_inc(to_dve.freed, dve.up(to_dve.freed))
            dve.wait_ge(to_dve.freed, dve.sent(to_dve.freed))

            def write_q(h, F):
                for par in range(2):
                    r_ = slice(64 * par, 64 * par + 64)
                    if h is None:
                        v.tensor_copy(gQ[r_, par], q[r_]).then_inc(dve_step, dve.up(dve_step))
                        dve.wait_ge(dve_step, dve.sent(dve_step))
                    else:
                        ins = v.tensor_tensor(halves(gQ[:, par], h, True)[0][r_], halves(q, h, True)[0][r_],
                                                     halves(F, h, True)[0][r_], ALU.mult)
                        ins.then_inc(dve_step, dve.up(dve_step))
                        dve.wait_ge(dve_step, dve.sent(dve_step))

            dve_levels(dve, gb, q, k, gF, write_q, gkF, [gatt[:, 0], gatt[:, 1]])
            dve.sem_inc(state_ready, dve.up(state_ready))
            for tt in range(2):
                for c in range(2):
                    r_ = slice(64 * c, 64 * c + 64)
                    dve.wait_ge(to_dve.filled, to_dve.next_filled())
                    bank = to_dve.filled_bank()
                    v.tensor_copy(br_tok[r_, tt], bank[r_, :]).then_inc(to_dve.freed, dve.up(to_dve.freed))
                    dve.wait_ge(to_dve.freed, dve.sent(to_dve.freed))
                    dve.wait_ge(to_dve.filled, to_dve.next_filled())
                    bank = to_dve.filled_bank()
                    e = P * tt + 64 * c + 63
                    for hp in range(2):
                        ins = v.scalar_tensor_tensor(out=gS[:, hp], in0=gS[:, hp], scalar=gE[:, hp * SEQ + e:hp * SEQ + e + 1],
                                                     in1=bank[:, hp * P:(hp + 1) * P], op0=ALU.mult, op1=ALU.add)
                        if hp:
                            ins.then_inc(to_dve.freed, dve.up(to_dve.freed))
                            dve.wait_ge(to_dve.freed, dve.sent(to_dve.freed))
                        else:
                            ins.then_inc(dve_step, dve.up(dve_step))
                            dve.wait_ge(dve_step, dve.sent(dve_step))
                    dve.sem_inc(state_ready, dve.up(state_ready))
                dve_norm_gate(dve, tt, 0, gla_gate[:, tt], gtmp2)

        def dve_norm_gate(dve, tt, which, gate, tmp):
            v = nc.vector
            y = br_tok[:, tt]
            y3 = y.rearrange("p (h n) -> p h n", h=4)
            dve_head_std(dve, y3, tmp.rearrange("p (h n) -> p h n", h=4), 4, P, HEAD_EPS)
            ins = v.tensor_tensor(y3, y3, normg[:, which:which + 1].broadcast_to([P, 4, P]), ALU.mult)
            ins.then_inc(dve_step, dve.up(dve_step))
            dve.wait_ge(dve_step, dve.sent(dve_step))
            v.tensor_tensor(y, y, gate, ALU.mult).then_inc(branch_ready, dve.up(branch_ready))
            dve.wait_ge(branch_ready, dve.sent(branch_ready))

        def pe_gla(pe):
            pe_gates(pe, 0)
            pe.wait_ge(kend_ready, pe.due(kend_ready))
            pe.wait_ge(to_dve.freed, to_dve.next_free())
            bank = to_dve.free_bank()
            for tt in range(2):
                for hp in range(2):
                    o = tt * 256 + hp * P
                    mm = pe.turn(bank[:, o:o + P], gkend[:, hp * SEQ + tt * P:hp * SEQ + (tt + 1) * P])
                    if tt and hp:
                        mm.then_inc(to_dve.filled, 1)

            def col(h, tt):
                o = (h // 2) * SEQ + tt * P
                return slice(o, o + P)

            late = {}

            def late_unit(l):
                tt, part = l // 2, l % 2
                if l == 0:
                    late["block"] = pe.block()
                if l < 4 and part == 0:
                    pe.wait_ge(to_act.freed, to_act.next_free())
                    late["bank"] = to_act.free_bank()
                if l < 4:
                    for k in range(KT):
                        mm = pe.mm(late["bank"][:, part * 256:(part + 1) * 256], x_lhs(k, tt),
                                   late["block"][:, k, part * 256:(part + 1) * 256], k == 0, k == KT - 1)
                        if k == 0:
                            pe.release(mm)
                        if part and k == KT - 1:
                            mm.then_inc(to_act.filled, 1)
                if l == 3:
                    pe.used()

            pe_levels(pe, lambda h, tt: gkF[:, col(h, tt)], lambda h, tt: gQ[:, h % 2, col(h, tt)],
                      [[(h, tt) for h in range(4)] for tt in range(2)], late_unit)
            for tt in range(2):
                for c in range(2):
                    r_ = slice(64 * c, 64 * c + 64)
                    pe.wait_ge(state_ready, pe.due(state_ready))
                    pe.wait_ge(to_dve.freed, to_dve.next_free())
                    bank = to_dve.free_bank()
                    for h in range(4):
                        hp, par = h // 2, h % 2
                        o = bank[r_, h * P:(h + 1) * P]
                        o0 = hp * SEQ + tt * P + 64 * c
                        pe.mm(o, gatt[:, tt, h, r_], gla_v[:, tt, h * P:(h + 1) * P], True, False)
                        mm = pe.mm(o, gQb[:, par, o0:o0 + 64], gS[:, hp], False, True)
                        if h == 3:
                            mm.then_inc(to_dve.filled, 1)
                    pe.wait_ge(to_dve.freed, to_dve.next_free())
                    bank = to_dve.free_bank()
                    for h in range(4):
                        hp, par = h // 2, h % 2
                        mm = pe.mm(bank[64 * par:64 * par + 64, hp * P:(hp + 1) * P], gktok[r_, tt, h * 64:(h + 1) * 64],
                                   gla_v[r_, tt, h * P:(h + 1) * P])
                        if h == 3:
                            mm.then_inc(to_dve.filled, 1)
            pe.wait_ge(state_ready, pe.due(state_ready))

        d = Bump(WORK + 12 * SEQ)
        cv = gdn_T
        dsq = d(8, SEQ)
        dv_tok = d(2, 512)
        dk_tok = d(2, 512)
        dG = d(2, 512)
        dbeta = d(2, 512)
        ddec = d(2, 4, P)
        dAT = d(2, 4, P)
        datt = d(2, 4, P)
        dSt = d(4, P)
        dsm = d(96)
        mm2 = Bump(WORK + 12 * SEQ)
        dT = mm2(8, P)
        dAm = mm2(8, P)
        dU = at(d.o, 8, P)
        assert d.o + 1024 <= arena_cols
        dX = at(WORK + 8 * SEQ, 512)
        dvn = at(WORK + 8 * SEQ + 512, 512)
        z_s, sp_s, g_s = dsm[:, 0:8], dsm[:, 8:16], dsm[:, 16:24]
        beta_s, G_s, eG_s = dsm[:, 24:32], dsm[:, 32:40], dsm[:, 40:48]
        kend_s, eend_s, ea_s, nbe_s = dsm[:, 48:56], dsm[:, 56:72], dsm[:, 72:76], dsm[:, 80:88]
        
        def two4(x):
            return x.rearrange("p (t h) -> p t h", t=2)

        def act_gdn(act):
            e = act.e
            act.wait_ge(softplus_in_ready, act.due(softplus_in_ready))
            e.activation(ea_s, ab_par[:, 0], ACT.Exp).then_inc(act_step, act.up(act_step))
            act.wait_ge(act_step, act.sent(act_step))
            e.activation(sp_s, sp_s, ACT.Exp, scale=-1.0).then_inc(act_step, act.up(act_step))
            act.wait_ge(act_step, act.sent(act_step))
            e.activation(sp_s, sp_s, ACT.Ln, bias=1.0).then_inc(softplus_log_ready, act.up(softplus_log_ready))
            act.wait_ge(softplus_log_ready, act.sent(softplus_log_ready))
            e.activation(two4(beta_s), gdn_ab[:, :, 4:8], ACT.Sigmoid).then_inc(beta_ready, act.up(beta_ready))
            act.wait_ge(beta_ready, act.sent(beta_ready))
            act_gates(act, 0)
            act.wait_ge(dss_ready, act.due(dss_ready))
            e.activation(dsq[:], dsq[:], ACT.Sqrt).then_inc(dnorm_ready, act.up(dnorm_ready))
            act.wait_ge(dnorm_ready, act.sent(dnorm_ready))
            act.wait_ge(dlog_ready, act.due(dlog_ready))
            e.activation(ddec[:], ddec[:], ACT.Exp).then_inc(act_step, act.up(act_step))
            act.wait_ge(act_step, act.sent(act_step))
            e.activation(eG_s, G_s, ACT.Exp).then_inc(act_step, act.up(act_step))
            act.wait_ge(act_step, act.sent(act_step))
            e.activation(kend_s, kend_s, ACT.Exp).then_inc(act_step, act.up(act_step))
            act.wait_ge(act_step, act.sent(act_step))
            e.activation(eend_s.rearrange("p (a c) -> p a c", c=2),
                                dG[:].rearrange("p t (h c n) -> p (t h) c n", h=4, c=2)[:, :, :, C - 1],
                                ACT.Exp).then_inc(ddecay_ready, act.up(ddecay_ready))
            act.wait_ge(ddecay_ready, act.sent(ddecay_ready))
            act_gates(act, 1)
            act_solve(act, dAm)
            for _ in range(2):
                act_head_std(act)

        def conv_slot(t):
            return xT[:, t % 8, SEQ:512]

        def dve_conv(dve):
            v = nc.vector
            for t in range(12):
                if t % 2 == 0:
                    dve.wait_ge(gdn_T_ready, dve.due(gdn_T_ready))
                if t >= 8:
                    dve.wait_ge(conv_silu_ready, dve.due(conv_silu_ready))
                x = gdn_T[:, t]
                y = conv_slot(t)

                def tap(i):
                    j = CONV + 12 * i + t
                    return cols[:, j:j + 1]

                v.tensor_scalar(y, x, tap(3), None, ALU.mult).then_inc(dve_step, dve.up(dve_step))
                dve.wait_ge(dve_step, dve.sent(dve_step))
                for s in (1, 2, 3):
                    ins = v.scalar_tensor_tensor(out=y[:, s:], in0=x[:, 0:SEQ - s], scalar=tap(3 - s), in1=y[:, s:],
                                                 op0=ALU.mult, op1=ALU.add)
                    done = conv_ready if s == 3 else dve_step
                    ins.then_inc(done, dve.up(done))
                    dve.wait_ge(done, dve.sent(done))
            dve.wait_ge(conv_silu_ready, dve.due(conv_silu_ready, 8))

        def act_conv(act, tiles):
            for t in tiles:
                act.wait_ge(conv_ready, act.due(conv_ready))
                ins = act.e.activation(cv[:, t], conv_slot(t), ACT.Silu)
                ins.then_inc(conv_silu_ready, act.up(conv_silu_ready))
                act.wait_ge(conv_silu_ready, act.sent(conv_silu_ready))

        def dve_gdn(dve):
            v = nc.vector
            dve.wait_ge(gdn_in_ready, dve.due(gdn_in_ready))
            ins = v.tensor_tensor(two4(z_s), gdn_ab[:, :, 0:4], ab_par[:, 1:2].broadcast_to([P, 2, 4]), ALU.add)
            ins.then_inc(dve_step, dve.up(dve_step))
            dve.wait_ge(dve_step, dve.sent(dve_step))
            ins = v.scalar_tensor_tensor(out=sp_s, in0=z_s, scalar=-1.0, in1=z_s, op0=ALU.mult, op1=ALU.max)
            ins.then_inc(softplus_in_ready, dve.up(softplus_in_ready))
            dve.wait_ge(softplus_in_ready, dve.sent(softplus_in_ready))
            dve.wait_ge(softplus_log_ready, dve.due(softplus_log_ready))
            ins = v.scalar_tensor_tensor(out=sp_s, in0=z_s, scalar=0.0, in1=sp_s, op0=ALU.max, op1=ALU.add)
            ins.then_inc(dve_step, dve.up(dve_step))
            dve.wait_ge(dve_step, dve.sent(dve_step))
            ins = (v.scalar_tensor_tensor(out=two4(g_s), in0=two4(sp_s), scalar=-1.0,
                                                in1=ea_s.unsqueeze(1).broadcast_to([P, 2, 4]), op0=ALU.mult, op1=ALU.mult))
            ins.then_inc(dve_step, dve.up(dve_step))
            dve.wait_ge(dve_step, dve.sent(dve_step))
            dve.wait_ge(beta_ready, dve.due(beta_ready))
            v.tensor_tensor(dsq[:], cv[:, 0:8], cv[:, 0:8], ALU.mult).then_inc(dve_step, dve.up(dve_step))
            dve.wait_ge(dve_step, dve.sent(dve_step))
            for tt in range(2):
                ins = v.tensor_copy(datt[:, tt], g_s[:, 4 * tt:4 * tt + 4].unsqueeze(2).broadcast_to([P, 4, P]))
                ins.then_inc(dve_step, dve.up(dve_step))
                dve.wait_ge(dve_step, dve.sent(dve_step))
                ins = v.tensor_copy(dAT[:, tt], beta_s[:, 4 * tt:4 * tt + 4].unsqueeze(2).broadcast_to([P, 4, P]))
                ins.then_inc(dve_step, dve.up(dve_step))
                dve.wait_ge(dve_step, dve.sent(dve_step))
            dve.sem_inc(dnorm_in_ready, dve.up(dnorm_in_ready))
            for gg in range(4):
                dve.wait_ge(to_dve.filled, to_dve.next_filled())
                bank = to_dve.filled_bank()
                v.tensor_scalar(dsq[:, 2 * gg:2 * gg + 2], bank[:].rearrange("p (a t) -> p a t", a=2),
                                                 1e-6, None, ALU.add).then_inc(to_dve.freed, dve.up(to_dve.freed))
                dve.wait_ge(to_dve.freed, dve.sent(to_dve.freed))
            dve.sem_inc(dss_ready, dve.up(dss_ready))
            dve.wait_ge(to_dve.filled, to_dve.next_filled())
            bank = to_dve.filled_bank()
            v.tensor_copy(G_s, bank[:, 0:8]).then_inc(to_dve.freed, dve.up(to_dve.freed))
            dve.wait_ge(to_dve.freed, dve.sent(to_dve.freed))
            for tt in range(2):
                dve.wait_ge(to_dve.filled, to_dve.next_filled())
                bank = to_dve.filled_bank()
                v.tensor_copy(dG[:, tt], bank[:]).then_inc(to_dve.freed, dve.up(to_dve.freed))
                dve.wait_ge(to_dve.freed, dve.sent(to_dve.freed))
                dve.wait_ge(to_dve.filled, to_dve.next_filled())
                bank = to_dve.filled_bank()
                v.tensor_copy(dbeta[:, tt], bank[:]).then_inc(to_dve.freed, dve.up(to_dve.freed))
                dve.wait_ge(to_dve.freed, dve.sent(to_dve.freed))
                ins = (v.tensor_tensor(ddec[:, tt], dG[:, tt].rearrange("p (h n) -> p h n", h=4),
                                             G_s[:, 4 * tt:4 * tt + 4].unsqueeze(2).broadcast_to([P, 4, P]), ALU.subtract))
                ins.then_inc(dve_step, dve.up(dve_step))
                dve.wait_ge(dve_step, dve.sent(dve_step))
                v.tensor_scalar(ddec[:, tt], ddec[:, tt], 0.0, None, ALU.min).then_inc(dve_step, dve.up(dve_step))
                dve.wait_ge(dve_step, dve.sent(dve_step))
                for c in range(2):
                    r_ = slice(64 * c, 64 * c + 64)
                    end = dG[:, tt].rearrange("p (h n) -> p h n", h=4)[r_, :, 64 * c + 63]
                    ins = v.tensor_tensor(kend_s[r_, 4 * tt:4 * tt + 4], end, G_s[r_, 4 * tt:4 * tt + 4], ALU.subtract)
                    ins.then_inc(dve_step, dve.up(dve_step))
                    dve.wait_ge(dve_step, dve.sent(dve_step))
            dve.sem_inc(dlog_ready, dve.up(dlog_ready))
            dve.wait_ge(dnorm_ready, dve.due(dnorm_ready))
            v.reciprocal(dsq[:], dsq[:]).then_inc(dve_step, dve.up(dve_step))
            dve.wait_ge(dve_step, dve.sent(dve_step))
            v.scalar_tensor_tensor(out=cv[:, 0:4], in0=cv[:, 0:4], scalar=float(P) ** -0.5, in1=dsq[:, 0:4],
                                          op0=ALU.mult, op1=ALU.mult).then_inc(dve_step, dve.up(dve_step))
            dve.wait_ge(dve_step, dve.sent(dve_step))
            v.tensor_tensor(cv[:, 4:8], cv[:, 4:8], dsq[:, 4:8], ALU.mult).then_inc(qk_ready, dve.up(qk_ready))
            dve.wait_ge(qk_ready, dve.sent(qk_ready))
            dve.wait_ge(ddecay_ready, dve.due(ddecay_ready))
            ins = v.scalar_tensor_tensor(out=nbe_s, in0=beta_s, scalar=-1.0, in1=eG_s, op0=ALU.mult, op1=ALU.mult)
            ins.then_inc(dve_step, dve.up(dve_step))
            dve.wait_ge(dve_step, dve.sent(dve_step))
            for tt in range(2):
                dve.wait_ge(to_dve.filled, to_dve.next_filled())
                bank = to_dve.filled_bank()
                ins = v.tensor_tensor(
                          dv_tok[:, tt].rearrange("p (h n) -> p h n", h=4), bank[:].rearrange("p (h n) -> p h n", h=4),
                          beta_s[:, 4 * tt:4 * tt + 4].unsqueeze(2).broadcast_to([P, 4, P]), ALU.mult)
                ins.then_inc(to_dve.freed, dve.up(to_dve.freed))
                dve.wait_ge(to_dve.freed, dve.sent(to_dve.freed))
                dve.wait_ge(to_dve.filled, to_dve.next_filled())
                bank = to_dve.filled_bank()
                v.tensor_copy(dk_tok[:, tt], bank[:]).then_inc(to_dve.freed, dve.up(to_dve.freed))
                dve.wait_ge(to_dve.freed, dve.sent(to_dve.freed))
                dve.wait_ge(to_dve.filled, to_dve.next_filled())
                bank = to_dve.filled_bank()
                v.tensor_tensor(dAT[:, tt], bank[:].rearrange("p (h n) -> p h n", h=4), ddec[:, tt],
                                                 ALU.mult).then_inc(to_dve.freed, dve.up(to_dve.freed))
                dve.wait_ge(to_dve.freed, dve.sent(to_dve.freed))
                ins = v.tensor_tensor(dAT[:, tt], dAT[:, tt], strictU.unsqueeze(1).broadcast_to([P, 4, P]), ALU.mult)
                ins.then_inc(dve_step, dve.up(dve_step))
                dve.wait_ge(dve_step, dve.sent(dve_step))
                at_flat = dAT[:, tt].rearrange("p h n -> p (h n)")
                v.scalar_tensor_tensor(out=at_flat, in0=dbeta[:, tt], scalar=-1.0, in1=at_flat, op0=ALU.mult,
                                              op1=ALU.mult).then_inc(dve_step, dve.up(dve_step))
                dve.wait_ge(dve_step, dve.sent(dve_step))
                dve.wait_ge(to_dve.filled, to_dve.next_filled())
                bank = to_dve.filled_bank()
                v.tensor_tensor(datt[:, tt], bank[:].rearrange("p (h n) -> p h n", h=4), ddec[:, tt],
                                                 ALU.mult).then_inc(to_dve.freed, dve.up(to_dve.freed))
                dve.wait_ge(to_dve.freed, dve.sent(to_dve.freed))
                ins = v.tensor_tensor(datt[:, tt], datt[:, tt], inclU.unsqueeze(1).broadcast_to([P, 4, P]), ALU.mult)
                ins.then_inc(dve_step, dve.up(dve_step))
                dve.wait_ge(dve_step, dve.sent(dve_step))
            for tt in range(2):
                dve_solve_start(dve, dU[:, 4 * tt:4 * tt + 4], dAT[:, tt])
            v.memset(dSt[:], 0.0).then_inc(dve_step, dve.up(dve_step))
            dve.wait_ge(dve_step, dve.sent(dve_step))
            v.memset(dX, 0.0).then_inc(dve_step, dve.up(dve_step))
            dve.wait_ge(dve_step, dve.sent(dve_step))
            v.memset(dvn, 0.0).then_inc(dve_step, dve.up(dve_step))
            dve.wait_ge(dve_step, dve.sent(dve_step))
            dve_solve(dve, lambda b: dAT[:, b], dT, dU, dAm)
            dve.sem_inc(state_ready, dve.up(state_ready))
            for tt in range(2):
                for c in range(2):
                    r_ = slice(64 * c, 64 * c + 64)
                    dve.wait_ge(to_dve.filled, to_dve.next_filled())
                    bank = to_dve.filled_bank()
                    for h in range(4):
                        s_ = slice(h * P, (h + 1) * P)
                        ins = v.scalar_tensor_tensor(out=dX[r_, s_], in0=bank[r_, s_],
                                                     scalar=nbe_s[r_, 4 * tt + h:4 * tt + h + 1], in1=dv_tok[r_, tt, s_],
                                                     op0=ALU.mult, op1=ALU.add)
                        if h == 3:
                            ins.then_inc(to_dve.freed, dve.up(to_dve.freed))
                            dve.wait_ge(to_dve.freed, dve.sent(to_dve.freed))
                        else:
                            ins.then_inc(dve_step, dve.up(dve_step))
                            dve.wait_ge(dve_step, dve.sent(dve_step))
                    dve.sem_inc(x_rows_ready, dve.up(x_rows_ready))
                    y3 = br_tok[r_, tt].rearrange("p (h n) -> p h n", h=4)
                    dve.wait_ge(to_dve.filled, to_dve.next_filled())
                    bank = to_dve.filled_bank()
                    v.tensor_tensor(y3, bank[r_, :].rearrange("p (h n) -> p h n", h=4),
                                                     eG_s[r_, 4 * tt:4 * tt + 4].unsqueeze(2).broadcast_to([64, 4, P]),
                                                     ALU.mult).then_inc(to_dve.freed, dve.up(to_dve.freed))
                    dve.wait_ge(to_dve.freed, dve.sent(to_dve.freed))
                    dve.wait_ge(to_dve.filled, to_dve.next_filled())
                    bank = to_dve.filled_bank()
                    v.tensor_copy(dvn[r_], bank[r_, :]).then_inc(dve_step, dve.up(dve_step))
                    dve.wait_ge(dve_step, dve.sent(dve_step))
                    ins = (v.tensor_tensor(
                              dX[r_].rearrange("p (h n) -> p h n", h=4), bank[r_, :].rearrange("p (h n) -> p h n", h=4),
                              kend_s[r_, 4 * tt:4 * tt + 4].unsqueeze(2).broadcast_to([64, 4, P]), ALU.mult))
                    ins.then_inc(to_dve.freed, dve.up(to_dve.freed))
                    dve.wait_ge(to_dve.freed, dve.sent(to_dve.freed))
                    dve.sem_inc(sa_ready, dve.up(sa_ready))
                    dve.wait_ge(to_dve.filled, to_dve.next_filled())
                    bank = to_dve.filled_bank()
                    ins = v.tensor_tensor(br_tok[r_, tt], bank[r_, :], br_tok[r_, tt], ALU.add)
                    ins.then_inc(to_dve.freed, dve.up(to_dve.freed))
                    dve.wait_ge(to_dve.freed, dve.sent(to_dve.freed))
                    dve.wait_ge(to_dve.filled, to_dve.next_filled())
                    bank = to_dve.filled_bank()
                    for h in range(4):
                        o = (4 * tt + h) * 2 + c
                        ins = v.scalar_tensor_tensor(out=dSt[:, h], in0=dSt[:, h], scalar=eend_s[:, o:o + 1],
                                                     in1=bank[:, h * P:(h + 1) * P], op0=ALU.mult, op1=ALU.add)
                        if h == 3:
                            ins.then_inc(to_dve.freed, dve.up(to_dve.freed))
                            dve.wait_ge(to_dve.freed, dve.sent(to_dve.freed))
                        else:
                            ins.then_inc(dve_step, dve.up(dve_step))
                            dve.wait_ge(dve_step, dve.sent(dve_step))
                    dve.sem_inc(state_ready, dve.up(state_ready))
                dve_norm_gate(dve, tt, 1, gdn_gate[:, tt], dG[:, 0] if tt else dbeta[:, 0])

        def pe_gdn(pe):
            pe_gates(pe, 0)
            pe.wait_ge(dnorm_in_ready, pe.due(dnorm_in_ready))
            for gg in range(4):
                pe.wait_ge(to_dve.freed, to_dve.next_free())
                bank = to_dve.free_bank()
                mm = pe.mm(bank[:], ones, dsq[:, 2 * gg:2 * gg + 2])
                mm.then_inc(to_dve.filled, 1)
            pe.wait_ge(to_dve.freed, to_dve.next_free())
            bank = to_dve.free_bank()
            for tt in range(2):
                mm = pe.mm(bank[:, 4 * tt:4 * tt + 4], inclU, g_s[:, 4 * tt:4 * tt + 4])
                if tt:
                    mm.then_inc(to_dve.filled, 1)
            for tt in range(2):
                pe.wait_ge(to_dve.freed, to_dve.next_free())
                bank = to_dve.free_bank()
                for h in range(4):
                    mm = pe.mm(bank[:, h * P:(h + 1) * P], datt[:, tt, h], inclU)
                    if h == 3:
                        mm.then_inc(to_dve.filled, 1)
                pe.wait_ge(to_dve.freed, to_dve.next_free())
                bank = to_dve.free_bank()
                for h in range(4):
                    mm = pe.mm(bank[:, h * P:(h + 1) * P], dAT[:, tt, h], ident)
                    if h == 3:
                        mm.then_inc(to_dve.filled, 1)
            pe_gates(pe, 1)
            pe.wait_ge(qk_ready, pe.due(qk_ready))
            for tt in range(2):
                toks = slice(tt * P, (tt + 1) * P)
                for t0 in (8, 4):
                    pe.wait_ge(to_dve.freed, to_dve.next_free())
                    bank = to_dve.free_bank()
                    for h in range(4):
                        mm = pe.turn(bank[:, h * P:(h + 1) * P], cv[:, t0 + h, toks])
                        if h == 3:
                            mm.then_inc(to_dve.filled, 1)
                for t0 in (4, 0):
                    pe.wait_ge(to_dve.freed, to_dve.next_free())
                    bank = to_dve.free_bank()
                    for h in range(4):
                        mm = pe.mm(bank[:, h * P:(h + 1) * P], cv[:, 4 + h, toks], cv[:, t0 + h, toks])
                        if h == 3:
                            mm.then_inc(to_dve.filled, 1)
            pe_solve(pe, dT, dU, dAm)
            for tt in range(2):
                for c in range(2):
                    r_ = slice(64 * c, 64 * c + 64)
                    ct = slice(tt * P + 64 * c, tt * P + 64 * c + 64)
                    pe.wait_ge(state_ready, pe.due(state_ready))
                    for t0 in (4, 0):
                        pe.wait_ge(to_dve.freed, to_dve.next_free())
                        bank = to_dve.free_bank()
                        for h in range(4):
                            mm = pe.mm(bank[r_, h * P:(h + 1) * P], cv[:, t0 + h, ct], dSt[:, h])
                            if h == 3:
                                mm.then_inc(to_dve.filled, 1)
                    pe.wait_ge(x_rows_ready, pe.due(x_rows_ready))
                    pe.wait_ge(to_dve.freed, to_dve.next_free())
                    bank = to_dve.free_bank()
                    for h in range(4):
                        mm = pe.mm(bank[r_, h * P:(h + 1) * P], dU[:, 4 * tt + h, r_], dX[:, h * P:(h + 1) * P])
                        if h == 3:
                            mm.then_inc(to_dve.filled, 1)
                    pe.wait_ge(sa_ready, pe.due(sa_ready))
                    pe.wait_ge(to_dve.freed, to_dve.next_free())
                    bank = to_dve.free_bank()
                    for h in range(4):
                        mm = pe.mm(bank[r_, h * P:(h + 1) * P], datt[:, tt, h, r_], dvn[:, h * P:(h + 1) * P])
                        if h == 3:
                            mm.then_inc(to_dve.filled, 1)
                    pe.wait_ge(to_dve.freed, to_dve.next_free())
                    bank = to_dve.free_bank()
                    for h in range(4):
                        s_ = slice(h * P, (h + 1) * P)
                        mm = pe.mm(bank[:, s_], dk_tok[r_, tt, s_], dX[r_, s_])
                        if h == 3:
                            mm.then_inc(to_dve.filled, 1)
            pe.wait_ge(state_ready, pe.due(state_ready))

        pl = Bump(FT * 512 + 1024)
        p_tok = pl(2, PLE)
        p_T = pl(2, SEQ)
        p_proj = pl(2, 2, 512)
        p_gate = pl(2, 2, 512)

        def pool_ple(pool, l):
            pool.e.dma_start(p_tok[:], a["p"][l, 0].rearrange("(t p) d -> p t d", p=P)).then_inc(p_landed, 16)

        def pe_ple(pe):
            pe.wait_ge(p_landed, pe.due(p_landed, 16))
            pe.wait_ge(to_act.freed, to_act.next_free())
            bank = to_act.free_bank()
            for k in range(2):
                for tt in range(2):
                    o = k * SEQ + tt * P
                    mm = pe.turn(bank[:, o:o + P], p_tok[:, tt, k * P:(k + 1) * P])
                    if k and tt:
                        mm.then_inc(to_act.filled, 1)
            pe.wait_ge(p_T_ready, pe.due(p_T_ready))
            blk = pe.block()
            wide2 = blk.rearrange("p k n -> p (k n)").rearrange("p (k n) -> p k n", n=D)
            for half in range(2):
                pe_tok(pe, wide2, to_act, half * 512, 512, lambda k, tt: p_T[:, k, tt * P:(tt + 1) * P], K=2)
            pe.used()
            pe.wait_ge(xT_ready, pe.due(xT_ready))
            for half in range(2):
                blk = pe.block()
                pe_tok(pe, blk, to_act, 0, 512, x_lhs)
                pe.used()

        def act_ple(act):
            act.wait_ge(to_act.filled, to_act.next_filled())
            bank = to_act.filled_bank()
            ins = act.e.copy(p_T[:], bank[:].rearrange("p (k t) -> p k t", k=2))
            ins.then_inc(to_act.freed, act.up(to_act.freed))
            act.wait_ge(to_act.freed, act.sent(to_act.freed))
            act.sem_inc(p_T_ready, act.up(p_T_ready))
            for dst, f in ((p_proj, ACT.Identity), (p_gate, ACT.Sigmoid)):
                for half in range(2):
                    for tt in range(2):
                        act.wait_ge(to_act.filled, to_act.next_filled())
                        bank = to_act.filled_bank()
                        act.e.activation(dst[:, half, tt], bank[:], f).then_inc(to_act.freed, act.up(to_act.freed))
                        act.wait_ge(to_act.freed, act.sent(to_act.freed))
            act.sem_inc(ple_ready, act.up(ple_ready))

        def dve_ple(dve):
            v = nc.vector
            dve.wait_ge(ple_ready, dve.due(ple_ready))
            for half in range(2):
                for tt in range(2):
                    x = xtok[:, tt, half * 512:(half + 1) * 512]
                    ins = v.tensor_tensor(p_gate[:, half, tt], p_gate[:, half, tt], p_proj[:, half, tt], ALU.mult)
                    ins.then_inc(dve_step, dve.up(dve_step))
                    dve.wait_ge(dve_step, dve.sent(dve_step))
                    v.tensor_tensor(x, x, p_gate[:, half, tt], ALU.add).then_inc(dve_step, dve.up(dve_step))
                    dve.wait_ge(dve_step, dve.sent(dve_step))

        HID = FT * 512 + 1024
        xn = at(HID, 2, 2, D)
        MIX_W, FFN_W, ADA_B = 0, 16, 32
        mod = modp[:, 0:DEPTH * 96].rearrange("p (l a s) -> p l a s", l=DEPTH, s=2)
        ccols = modp[:, 192:208]
        Amod = modp[:, 208:272].rearrange("p (l w k s) -> p l w k s", l=DEPTH, w=2, k=KT)
        lbc = modp[:, 272:304]
        lb, omlb = lbc[:, 0:8], lbc[:, 8:16]
        stream_tok = (xtok, ctok)
        SH1, SC1, GT1, SH2, SC2, GT2 = range(6)

        ADA_BLOCKS = DEPTH * 6 * D // 512
        ADA_STEP = ADA_BLOCKS // (4 * DEPTH)

        ada_rows = at(arena_cols - 2 * 512, 2, 512)

        def ada_steps():
            steps = []
            for i in range(ADA_STEP):
                steps.append(("product", i))
                if i:
                    steps.append(("turn", i - 1))
            return steps + [("turn", ADA_STEP - 1)]

        def pe_ada(pe):
            for step, i in ada_steps():
                if step == "product":
                    blk = pe.block()
                    pe.wait_ge(to_act.freed, to_act.next_free())
                    bank = to_act.free_bank()
                    for k in range(KT):
                        mm = pe.mm(bank[0:2, :], ccols[:, k:16:8], blk[:, k, :], k == 0, k == KT - 1)
                        if k == 0:
                            pe.release(mm)
                        if k == KT - 1:
                            mm.then_inc(to_act.filled, 1)
                    pe.used()
                else:
                    pe.wait_ge(ada_rows_ready, pe.due(ada_rows_ready))
                    pe.wait_ge(to_act.freed, to_act.next_free())
                    bank = to_act.free_bank()
                    for j in range(4):
                        mm = pe.turn(bank[:, 2 * j:2 * j + 2], ada_rows[0:2, i % 2, j * P:(j + 1) * P], 2)
                        if j == 3:
                            mm.then_inc(to_act.filled, 1)

        def act_ada(act, step, i):
            act.wait_ge(to_act.filled, to_act.next_filled())
            bank = to_act.filled_bank()
            if step == "product":
                act.e.copy(ada_rows[0:2, i % 2], bank[0:2, :]).then_inc(to_act.freed, act.up(to_act.freed))
                act.wait_ge(to_act.freed, act.sent(to_act.freed))
                act.sem_inc(ada_rows_ready, act.up(ada_rows_ready))
            else:
                n = act.ada
                act.e.copy(modp[:, 8 * n:8 * n + 8], bank[:, 0:8]).then_inc(to_act.freed, act.up(to_act.freed))
                act.wait_ge(to_act.freed, act.sent(to_act.freed))
                act.ada += 1

        def pe_turn_c(pe):
            pe.wait_ge(c_landed, pe.due(c_landed, 32))
            pe.wait_ge(to_act.freed, to_act.next_free())
            bank = to_act.free_bank()
            mm = pe.turn(bank[:, 0:16], rows[0:16, :], 16)
            mm.then_inc(to_act.filled, 1)

        def act_turn_c(act):
            act.wait_ge(to_act.filled, to_act.next_filled())
            bank = to_act.filled_bank()
            act.e.activation(ccols, bank[:, 0:16], ACT.Silu).then_inc(to_act.freed, act.up(to_act.freed))
            act.wait_ge(to_act.freed, act.sent(to_act.freed))
            act.sem_inc(c_cols_ready, act.up(c_cols_ready))

        def act_first_loads(act):
            act.e.dma_start(rows[0:8, :], a["c_2"][0].rearrange("(r p) -> r p", p=P)).then_inc(c_landed, 16)
            act.e.dma_start(rows[8:16, :], a["c_ctx_2"].rearrange("(r p) -> r p", p=P)).then_inc(c_landed, 16)
            act.e.dma_start(xtok[:], a["x"][0].rearrange("(t p) d -> p t d", p=P)).then_inc(x_landed, 16)

        def pe_norm_mod(pe, streams):
            for s in streams:
                pe.wait_ge(xn_ready, pe.due(xn_ready))
                for q in range(4):
                    pe.wait_ge(to_act.freed, to_act.next_free())
                    bank = to_act.free_bank()
                    for j in range(2):
                        for tt in range(2):
                            kt = 2 * q + j
                            o = j * SEQ + tt * P
                            mm = pe.turn(bank[:, o:o + P], xn[:, s, tt, kt * P:(kt + 1) * P])
                            if j and tt:
                                mm.then_inc(to_act.filled, 1)

        def act_norm_mod(act, l, which, streams):
            for s in streams:
                for tt in range(2):
                    act.wait_ge(var_ready, act.due(var_ready))
                    act.e.activation(small[:, 3:4], small[:, 2:3], ACT.Sqrt).then_inc(std_ready, act.up(std_ready))
                    act.wait_ge(std_ready, act.sent(std_ready))
            for s in streams:
                for q in range(4):
                    act.wait_ge(to_act.filled, to_act.next_filled())
                    bank = to_act.filled_bank()
                    for j in range(2):
                        kt = 2 * q + j
                        sh = mod[:, l, (SH1, SH2)[which] * KT + kt, s:s + 1]
                        ins = act.e.activation(xT[:, kt, s * SEQ:(s + 1) * SEQ], bank[:, j * SEQ:(j + 1) * SEQ],
                                               ACT.Identity, scale=Amod[:, l, which, kt, s:s + 1], bias=sh)
                        if j:
                            ins.then_inc(to_act.freed, act.up(to_act.freed))
                            act.wait_ge(to_act.freed, act.sent(to_act.freed))
                        else:
                            ins.then_inc(act_step, act.up(act_step))
                            act.wait_ge(act_step, act.sent(act_step))
            act.sem_inc(xT_ready, act.up(xT_ready))

        def dve_rstd(dve, x, tmp):
            v = nc.vector
            v.tensor_tensor(tmp, x, x, ALU.mult).then_inc(dve_step, dve.up(dve_step))
            dve.wait_ge(dve_step, dve.sent(dve_step))
            v.tensor_reduce(small[:, 1:2], tmp, AX.X, ALU.add).then_inc(dve_step, dve.up(dve_step))
            dve.wait_ge(dve_step, dve.sent(dve_step))
            ins = v.tensor_scalar(small[:, 2:3], small[:, 1:2], 1.0 / D, HEAD_EPS, ALU.mult, ALU.add)
            ins.then_inc(var_ready, dve.up(var_ready))
            dve.wait_ge(var_ready, dve.sent(var_ready))
            dve.wait_ge(std_ready, dve.due(std_ready))
            v.reciprocal(small[:, 4:5], small[:, 3:4]).then_inc(dve_step, dve.up(dve_step))
            dve.wait_ge(dve_step, dve.sent(dve_step))

        def dve_norm_tile(dve, s, tt):
            x = stream_tok[s][:, tt]
            dve_rstd(dve, x, xn[:, s, tt])
            ins = nc.vector.tensor_scalar(xn[:, s, tt], x, small[:, 4:5], None, ALU.mult)
            ins.then_inc(dve_step, dve.up(dve_step))
            dve.wait_ge(dve_step, dve.sent(dve_step))
            if tt:
                dve.sem_inc(xn_ready, dve.up(xn_ready))

        def dve_norm_mod(dve, streams):
            for s in streams:
                for tt in range(2):
                    dve_norm_tile(dve, s, tt)

        def dve_gate_rows(dve, l, which, streams, diag):
            v = nc.vector
            for s in streams:
                for q in range(2):
                    for k in range(4):
                        kt = 4 * q + k
                        v.tensor_scalar(diag[:, k * P:(k + 1) * P], ident, mod[:, l, which * KT + kt, s:s + 1], None,
                                               ALU.mult).then_inc(dve_step, dve.up(dve_step))
                        dve.wait_ge(dve_step, dve.sent(dve_step))
                    dve.sem_inc(diag_ready, dve.up(diag_ready))
                    dve.wait_ge(to_dve.filled, to_dve.next_filled())
                    bank = to_dve.filled_bank()
                    ins = v.tensor_copy(lnp[:, s, q * 512:(q + 1) * 512], bank[:])
                    ins.then_inc(to_dve.freed, dve.up(to_dve.freed))
                    dve.wait_ge(to_dve.freed, dve.sent(to_dve.freed))

        def pe_gate_rows(pe, streams, diag):
            for s in streams:
                for q in range(2):
                    pe.wait_ge(diag_ready, pe.due(diag_ready))
                    pe.wait_ge(to_dve.freed, to_dve.next_free())
                    bank = to_dve.free_bank()
                    mm = pe.mm(bank[:], ones, diag)
                    mm.then_inc(to_dve.filled, 1)

        def dve_gated_residual(dve, streams, tmp, norm=True):
            v = nc.vector
            for half in range(2):
                c_ = slice(half * 512, (half + 1) * 512)
                for s in streams:
                    for tt in range(2):
                        dve.wait_ge(to_dve.filled, to_dve.next_filled())
                        bank = to_dve.filled_bank()
                        x = stream_tok[s][:, tt, c_]
                        ins = v.tensor_tensor(tmp, bank[:], lnp[:, s, c_], ALU.mult)
                        ins.then_inc(to_dve.freed, dve.up(to_dve.freed))
                        dve.wait_ge(to_dve.freed, dve.sent(to_dve.freed))
                        v.tensor_tensor(x, x, tmp, ALU.add).then_inc(dve_step, dve.up(dve_step))
                        dve.wait_ge(dve_step, dve.sent(dve_step))
                        if norm and half:
                            dve_norm_tile(dve, s, tt)

        gtmp_row = at(HID + 4 * D, 512)
        diag = at(HID + 4 * D + 512, 512)

        t = Bump(0)
        QKH = 20
        oT = t(8, 512)
        qk_tok = t(4, QKH * 64)
        av_tok = t(4, 256)
        kz = t(8, P)
        kTz = t(8, 512)
        qT = xT
        Pb = t(2, 2, 512)
        PT = t(2, 4, SEQ)
        asq = at(t.o, QKH * 64)
        rope_t = Pb[:].rearrange("p a b c -> p (a b c)")
        qkn = at(t.o + QKH * 64, 2, 64)
        am = at(t.o + QKH * 64 + P, 64)
        adiag = at(t.o + QKH * 64 + P + 64, 512)

        def pe_attention(pe):
            pe.wait_ge(xT_ready, pe.due(xT_ready))
            blks = []
            for tt in range(5):
                for b in range(3 if tt < 4 else 0):
                    if tt == 0:
                        blks.append(pe.block())
                    pe_tok(pe, blks[b], to_act, 0, 512, x_lhs, (tt,))
                if tt == 3:
                    for _ in range(3):
                        pe.used()
                if tt == 0:
                    pe_gate_rows(pe, (0, 1), adiag)
                    continue
                pe.wait_ge(qk_tile_ready, pe.due(qk_tile_ready))
                for src, n in ((qk_tok[:, tt - 1], 2), (kz[:].rearrange("p a b -> p (a b)"), 2)):
                    for q in range(n):
                        pe.wait_ge(to_act.freed, to_act.next_free())
                        bank = to_act.free_bank()
                        for k in range(4):
                            o = (4 * q + k) * P
                            mm = pe.turn(bank[:, k * P:(k + 1) * P], src[:, o:o + P])
                            if k == 0:
                                pe.release(mm)
                            if k == 3:
                                mm.then_inc(to_act.filled, 1)
            pe.wait_ge(qkT_ready, pe.due(qkT_ready))
            units = attention_units()
            score_banks.clear()

            def scores(u):
                h, s = units[u]
                kvp = 2 * (h // 4) + h % 2
                if s == 0:
                    for qt in range(2):
                        pe.wait_ge(to_act.freed, to_act.next_free())
                        bank = to_act.free_bank()
                        score_banks.append((to_act.opened, bank))
                        mm = pe.mm(bank[:], qT[:, h // 2, qt * P:(qt + 1) * P], kTz[:, kvp])
                        mm.then_inc(to_act.filled, 1)
                else:
                    pe.wait_ge(to_act.freed, to_act.next_free())
                    bank = to_act.free_bank()
                    score_banks.append((to_act.opened, bank))
                    for qt in range(2):
                        mm = pe.mm(bank[:, qt * SEQ:(qt + 1) * SEQ], qT[:, h // 2, SEQ + qt * P:SEQ + (qt + 1) * P],
                                   kTz[:, kvp, SEQ:512])
                        if qt:
                            mm.then_inc(to_act.filled, 1)

            def turn_probs(u):
                h, s = units[u]
                pe.wait_ge(probs_scaled, pe.due(probs_scaled))
                nk = 4 if s == 0 else 2
                for k0 in range(0, nk, 2):
                    pe.wait_ge(to_act.freed, to_act.next_free())
                    bank = to_act.free_bank()
                    for k in range(k0, k0 + 2):
                        for qt in range(2):
                            o = (k - k0) * SEQ + qt * P
                            src = Pb[:, u % 2, qt, k * P:(k + 1) * P] if s == 0 else \
                                Pb[:, u % 2, 0, qt * SEQ + k * P:qt * SEQ + (k + 1) * P]
                            mm = pe.turn(bank[:, o:o + P], src)
                            if k > k0 and qt:
                                mm.then_inc(to_act.filled, 1)

            def weigh(u):
                h, s = units[u]
                pe.wait_ge(PT_ready, pe.due(PT_ready))
                nk = 4 if s == 0 else 2
                par = h % 2
                pe.wait_ge(to_dve.freed, to_dve.next_free())
                bank = to_dve.free_bank()
                for k in range(nk):
                    tt = k if s == 0 else 2 + k
                    mm = pe.mm(bank[64 * par:64 * par + 64, 0:SEQ], av_tok[:, tt, (h // 4) * 64:(h // 4 + 1) * 64],
                               PT[:, u % 2, k], k == 0, k == nk - 1)
                    if k == nk - 1:
                        mm.then_inc(to_dve.filled, 1)

            for u in range(len(units) + 2):
                if u < len(units):
                    scores(u)
                if 1 <= u <= len(units):
                    turn_probs(u - 1)
                if u >= 2:
                    weigh(u - 2)
            pe.wait_ge(oT_ready, pe.due(oT_ready))
            for half in range(2):
                blk = pe.block()
                pe_tok(pe, blk, to_dve, 0, 512, lambda k, tt: oT[:, k, tt * P:(tt + 1) * P], (0, 1, 2, 3))
                pe.used()

        score_banks = []

        def attention_units():
            return [(h, s) for s in range(2) for h in range(16)]

        def act_attention(act):
            e = act.e
            for tt in range(5):
                if tt < 4:
                    for half in range(2):
                        act.wait_ge(to_act.filled, to_act.next_filled())
                        bank = to_act.filled_bank()
                        ins = e.copy(qk_tok[:, tt, half * 512:(half + 1) * 512], bank[:])
                        ins.then_inc(to_act.freed, act.up(to_act.freed))
                        act.wait_ge(to_act.freed, act.sent(to_act.freed))
                    act.wait_ge(to_act.filled, to_act.next_filled())
                    bank = to_act.filled_bank()
                    e.copy(qk_tok[:, tt, 1024:1280], bank[:, 0:256]).then_inc(act_step, act.up(act_step))
                    act.wait_ge(act_step, act.sent(act_step))
                    e.copy(av_tok[:, tt], bank[:, 256:512]).then_inc(to_act.freed, act.up(to_act.freed))
                    act.wait_ge(to_act.freed, act.sent(to_act.freed))
                    act.sem_inc(qkv_ready, act.up(qkv_ready))
                if tt:
                    for dst in (qT, kTz):
                        for q in range(2):
                            act.wait_ge(to_act.filled, to_act.next_filled())
                            bank = to_act.filled_bank()
                            ins = e.copy(dst[:, 4 * q:4 * q + 4, (tt - 1) * P:tt * P],
                                         bank[:].rearrange("p (k t) -> p k t", k=4))
                            ins.then_inc(to_act.freed, act.up(to_act.freed))
                            act.wait_ge(to_act.freed, act.sent(to_act.freed))
                    act.sem_inc(qk_tile_turned, act.up(qk_tile_turned))
                if tt < 4:
                    act.wait_ge(qk_var_ready, act.due(qk_var_ready))
                    e.activation(am[:, 0:20], am[:, 0:20], ACT.Sqrt).then_inc(qk_std_ready, act.up(qk_std_ready))
                    act.wait_ge(qk_std_ready, act.sent(qk_std_ready))
            act.sem_inc(qkT_ready, act.up(qkT_ready))
            units = attention_units()

            def exps(u):
                h, s = units[u]
                act.wait_ge(max_ready, act.due(max_ready))
                if s == 0:
                    for qt in range(2):
                        act.wait_ge(to_act.filled, to_act.next_filled())
                        bank = to_act.filled_bank()
                        ins = e.activation(Pb[:, u % 2, qt], bank[:], ACT.Exp, scale=0.125,
                                           bias=am[:, 4 * (u % 2) + 2 + qt:4 * (u % 2) + 3 + qt],
                                           accum_out=am[:, 8 + 2 * (u % 2) + qt:9 + 2 * (u % 2) + qt])
                        ins.then_inc(to_act.freed, act.up(to_act.freed))
                        act.wait_ge(to_act.freed, act.sent(to_act.freed))
                else:
                    act.wait_ge(to_act.filled, to_act.next_filled())
                    bank = to_act.filled_bank()
                    for qt in range(2):
                        ins = e.activation(Pb[:, u % 2, 0, qt * SEQ:(qt + 1) * SEQ], bank[:, qt * SEQ:(qt + 1) * SEQ],
                                           ACT.Exp, scale=0.125,
                                           bias=am[:, 4 * (u % 2) + 2 + qt:4 * (u % 2) + 3 + qt],
                                           accum_out=am[:, 8 + 2 * (u % 2) + qt:9 + 2 * (u % 2) + qt])
                        if qt:
                            ins.then_inc(to_act.freed, act.up(to_act.freed))
                            act.wait_ge(to_act.freed, act.sent(to_act.freed))
                        else:
                            ins.then_inc(act_step, act.up(act_step))
                            act.wait_ge(act_step, act.sent(act_step))
                act.sem_inc(probs_ready, act.up(probs_ready))

            def keep_PT(u):
                h, s = units[u]
                for k0 in range(0, 4 if s == 0 else 2, 2):
                    act.wait_ge(to_act.filled, to_act.next_filled())
                    bank = to_act.filled_bank()
                    ins = e.copy(PT[:, u % 2, k0:k0 + 2], bank[:].rearrange("p (k t) -> p k t", k=2))
                    ins.then_inc(to_act.freed, act.up(to_act.freed))
                    act.wait_ge(to_act.freed, act.sent(to_act.freed))
                act.sem_inc(PT_ready, act.up(PT_ready))

            for u in range(len(units) + 1):
                if u < len(units):
                    exps(u)
                if u >= 1:
                    keep_PT(u - 1)

        def dve_attention(dve):
            v = nc.vector
            v.memset(kz[:], 0.0).then_inc(dve_step, dve.up(dve_step))
            dve.wait_ge(dve_step, dve.sent(dve_step))
            dve_gate_rows(dve, 0, GT1, (0, 1), adiag)
            dve.wait_ge(qk_norm_landed, dve.due(qk_norm_landed, 32))
            for tt in range(4):
                dve.wait_ge(qkv_ready, dve.due(qkv_ready))
                x = qk_tok[:, tt].rearrange("p (h n) -> p h n", n=64)
                sq3 = asq.rearrange("p (h n) -> p h n", n=64)
                v.tensor_tensor(sq3, x, x, ALU.mult).then_inc(dve_step, dve.up(dve_step))
                dve.wait_ge(dve_step, dve.sent(dve_step))
                v.tensor_reduce(am[:, 0:20], sq3, AX.X, ALU.add).then_inc(dve_step, dve.up(dve_step))
                dve.wait_ge(dve_step, dve.sent(dve_step))
                ins = v.tensor_scalar(am[:, 0:20], am[:, 0:20], 1.0 / 64, 1e-6, ALU.mult, ALU.add)
                ins.then_inc(qk_var_ready, dve.up(qk_var_ready))
                dve.wait_ge(qk_var_ready, dve.sent(qk_var_ready))
                dve.wait_ge(qk_std_ready, dve.due(qk_std_ready))
                v.reciprocal(am[:, 20:40], am[:, 0:20]).then_inc(dve_step, dve.up(dve_step))
                dve.wait_ge(dve_step, dve.sent(dve_step))
                ins = v.tensor_tensor(x, x, am[:, 20:40].unsqueeze(2).broadcast_to([P, QKH, 64]), ALU.mult)
                ins.then_inc(dve_step, dve.up(dve_step))
                dve.wait_ge(dve_step, dve.sent(dve_step))
                ins = v.tensor_tensor(x[:, 0:16], x[:, 0:16], qkn[:, 0:1].broadcast_to([P, 16, 64]), ALU.mult)
                ins.then_inc(dve_step, dve.up(dve_step))
                dve.wait_ge(dve_step, dve.sent(dve_step))
                ins = v.tensor_tensor(x[:, 16:20], x[:, 16:20], qkn[:, 1:2].broadcast_to([P, 4, 64]), ALU.mult)
                ins.then_inc(dve_step, dve.up(dve_step))
                dve.wait_ge(dve_step, dve.sent(dve_step))
                if tt < 2:
                    x5 = qk_tok[:, tt].rearrange("p (h x e n) -> p h x e n", x=2, e=2, n=16)
                    x1, x2 = x5[:, :, :, 0], x5[:, :, :, 1]
                    n = QKH * 32

                    def table(i):
                        o = (2 * tt + i) * 32
                        return rope[:, o:o + 32].rearrange("p (x n) -> p x n", x=2).unsqueeze(1).broadcast_to([P, QKH, 2, 16])

                    def tmp(i):
                        return (rope_t[:, i * n:(i + 1) * n] if i < 3 else asq[:, 0:n]).rearrange(
                            "p (h x n) -> p h x n", x=2, n=16)

                    v.tensor_tensor(tmp(0), x1, table(0), ALU.mult).then_inc(dve_step, dve.up(dve_step))
                    dve.wait_ge(dve_step, dve.sent(dve_step))
                    v.tensor_tensor(tmp(1), x2, table(1), ALU.mult).then_inc(dve_step, dve.up(dve_step))
                    dve.wait_ge(dve_step, dve.sent(dve_step))
                    v.tensor_tensor(tmp(2), x2, table(0), ALU.mult).then_inc(dve_step, dve.up(dve_step))
                    dve.wait_ge(dve_step, dve.sent(dve_step))
                    v.tensor_tensor(tmp(3), x1, table(1), ALU.mult).then_inc(dve_step, dve.up(dve_step))
                    dve.wait_ge(dve_step, dve.sent(dve_step))
                    v.tensor_tensor(x1, tmp(0), tmp(1), ALU.subtract).then_inc(dve_step, dve.up(dve_step))
                    dve.wait_ge(dve_step, dve.sent(dve_step))
                    v.tensor_tensor(x2, tmp(2), tmp(3), ALU.add).then_inc(dve_step, dve.up(dve_step))
                    dve.wait_ge(dve_step, dve.sent(dve_step))
                if tt:
                    dve.wait_ge(qk_tile_turned, dve.due(qk_tile_turned))
                kzv = kz[:].rearrange("p (g r) n -> p g r n", r=2)
                for par in range(2):
                    ins = v.tensor_copy(kzv[:, :, par, 64 * par:64 * par + 64], x[:, 16:20])
                    ins.then_inc(dve_step, dve.up(dve_step))
                    dve.wait_ge(dve_step, dve.sent(dve_step))
                dve.sem_inc(qk_tile_ready, dve.up(qk_tile_ready))
            dve.wait_ge(qk_tile_turned, dve.due(qk_tile_turned))
            units = attention_units()
            banks = list(score_banks)

            def maxes(u):
                h, s = units[u]
                o = 4 * (u % 2)
                if s == 0:
                    for qt in range(2):
                        n, bank = banks.pop(0)
                        dve.wait_ge(to_act.filled, n)
                        ins = v.tensor_reduce(am[:, o + qt:o + qt + 1], bank[:], AX.X, ALU.max)
                        ins.then_inc(dve_step, dve.up(dve_step))
                        dve.wait_ge(dve_step, dve.sent(dve_step))
                else:
                    n, bank = banks.pop(0)
                    dve.wait_ge(to_act.filled, n)
                    ins = v.tensor_reduce(am[:, o:o + 2], bank[:].rearrange("p (a b) -> p a b", a=2), AX.X, ALU.max)
                    ins.then_inc(dve_step, dve.up(dve_step))
                    dve.wait_ge(dve_step, dve.sent(dve_step))
                ins = v.tensor_scalar(am[:, o + 2:o + 4], am[:, o:o + 2], -0.125, None, ALU.mult)
                ins.then_inc(max_ready, dve.up(max_ready))
                dve.wait_ge(max_ready, dve.sent(max_ready))

            def scale(u):
                h, s = units[u]
                dve.wait_ge(probs_ready, dve.due(probs_ready))
                o = 2 * (u % 2)
                r = am[:, 12 + o:14 + o]
                v.reciprocal(r, am[:, 8 + o:10 + o]).then_inc(dve_step, dve.up(dve_step))
                dve.wait_ge(dve_step, dve.sent(dve_step))
                for qt in range(2):
                    pv = Pb[:, u % 2, qt] if s == 0 else Pb[:, u % 2, 0, qt * SEQ:(qt + 1) * SEQ]
                    ins = v.tensor_scalar(pv, pv, r[:, qt:qt + 1], None, ALU.mult)
                    if qt:
                        ins.then_inc(probs_scaled, dve.up(probs_scaled))
                        dve.wait_ge(probs_scaled, dve.sent(probs_scaled))
                    else:
                        ins.then_inc(dve_step, dve.up(dve_step))
                        dve.wait_ge(dve_step, dve.sent(dve_step))

            def keep_o(u):
                h, s = units[u]
                par = h % 2
                r_ = slice(64 * par, 64 * par + 64)
                dve.wait_ge(to_dve.filled, to_dve.next_filled())
                bank = to_dve.filled_bank()
                ins = v.tensor_copy(oT[r_, h // 2, s * SEQ:(s + 1) * SEQ], bank[r_, 0:SEQ])
                ins.then_inc(to_dve.freed, dve.up(to_dve.freed))
                dve.wait_ge(to_dve.freed, dve.sent(to_dve.freed))

            for u in range(len(units) + 3):
                if u < len(units):
                    maxes(u)
                if u >= 3:
                    keep_o(u - 3)
                if u < len(units):
                    scale(u)
            dve.sem_inc(oT_ready, dve.up(oT_ready))
            dve_gated_residual(dve, (0, 1), gtmp_row)

        u = Bump(0)
        hz = [u(2, KT, SEQ), u(2, KT, SEQ)]
        hv = u(4, D)
        hq = u(KT, SEQ)
        hgate = u(2, D)
        hF = u(KT * SEQ)
        hQ = u(KT * SEQ)
        hkF = u(KT * SEQ)
        hatt = u(16, P)
        hS = u(KT, P)
        hend = u(KT, 4)
        xT_halves = xT[:].rearrange("p k t -> p (k t)").rearrange("p (s k t) -> p s k t", s=2, k=KT)
        hk = [[ctok[:].rearrange("p a b -> p (a b)").rearrange("p (k t) -> p k t", k=KT),
               hgate.rearrange("p a b -> p (a b)").rearrange("p (k t) -> p k t", k=KT)],
              [xT_halves[:, 0], xT_halves[:, 1]]]
        ho = ctok
        h_tmp = hF[:, 0:D]
        hdiag = hQ[:, 0:512]
        hrow_tmp = hQ[:, 512:1024]
        lvl_batches = [[(h, tt) for h in range(4 * b, 4 * b + 4)] for tt in range(2) for b in range(2)]

        def flat(x):
            return x.rearrange("p k t -> p (k t)")

        def pe_hgrn(pe):
            pe.wait_ge(xT_ready, pe.due(xT_ready))
            for b in range(2):
                blk = pe.block()
                pe_T(pe, blk, to_act, 0, [P] * 4, 512)
                pe.used()
                if b == 0:
                    pe_gate_rows(pe, (0,), hdiag)
            for _ in range(2):
                blk = pe.block()
                pe_tok(pe, blk, to_act, 0, 512, x_lhs, (0, 1, 2, 3))
                pe.used()
            for _ in range(2):
                blk = pe.block()
                pe_T(pe, blk, to_act, 0, [P] * 4)
                pe.used()
            late = [None]

            def late_unit(u):
                per = 4 if u < 8 else 2
                if u % per == 0:
                    late[0] = pe.block()
                if u < 8:
                    pe_T(pe, late[0], to_act, u % 4 * P, [P], 512)
                else:
                    pe_tok(pe, late[0], to_act, 0, 512, x_lhs, (u % 2,))
                if u % per == per - 1:
                    pe.used()

            for back in range(2):
                pe.wait_ge(ctx_keys_ready, pe.due(ctx_keys_ready))
                pe_turn_heads(pe, hQ)
                pe.wait_ge(key_tok_ready, pe.due(key_tok_ready))
                kt3 = hkF.rearrange("p (t n) -> p t n", t=2)
                for b in range(2):
                    pe.wait_ge(to_dve.freed, to_dve.next_free())
                    bank = to_dve.free_bank()
                    for j in range(4):
                        h = 4 * b + j
                        s_ = slice(h * P, (h + 1) * P)
                        for tt in range(2):
                            mm = pe.mm(bank[:, j * P:(j + 1) * P], kt3[:, tt, s_],
                                       hv[:, 2 + tt, s_], tt == 0, tt == 1)
                            if j == 3 and tt:
                                mm.then_inc(to_dve.filled, 1)

                def at_(x):
                    return lambda h, tt: x[:, h * SEQ + tt * P:h * SEQ + (tt + 1) * P]

                pe_levels(pe, at_(hkF), at_(hQ), lvl_batches, None if back else late_unit)
                if not back:
                    late_unit(7)
                    late_unit(8)
                pe.wait_ge(kend_ready, pe.due(kend_ready))
                pe_turn_heads(pe, hkF)
                kt3 = hF.rearrange("p (t n) -> p t n", t=2)
                for i in range(4):
                    n = 3 - i if back else i
                    tt, c = n // 2, n % 2
                    r_ = slice(64 * c, 64 * c + 64)
                    if not back and i:
                        late_unit(8 + i)
                    pe.wait_ge(state_ready, pe.due(state_ready))
                    for b in range(2):
                        pe.wait_ge(to_dve.freed, to_dve.next_free())
                        bank = to_dve.free_bank()
                        for j in range(4):
                            h = 4 * b + j
                            s_ = slice(h * P, (h + 1) * P)
                            o = bank[r_, j * P:(j + 1) * P]
                            pe.mm(o, hatt[:, tt * KT + h, r_], hv[:, tt, s_], True, False)
                            q0 = h * SEQ + n * C
                            mm = pe.mm(o, hQ[:, q0:q0 + C], hS[:, h], False, True)
                            if j == 3:
                                mm.then_inc(to_dve.filled, 1)
                    for b in range(2):
                        pe.wait_ge(to_dve.freed, to_dve.next_free())
                        bank = to_dve.free_bank()
                        for j in range(4):
                            s_ = slice((4 * b + j) * P, (4 * b + j + 1) * P)
                            mm = pe.mm(bank[:, j * P:(j + 1) * P], kt3[r_, tt, s_], hv[r_, tt, s_])
                            if j == 3:
                                mm.then_inc(to_dve.filled, 1)
                pe.wait_ge(state_ready, pe.due(state_ready))
            for tt in range(2):
                pe.wait_ge(readout_ready, pe.due(readout_ready))
                for q in range(2):
                    pe.wait_ge(to_act.freed, to_act.next_free())
                    bank = to_act.free_bank()
                    for k in range(4):
                        kt = 4 * q + k
                        mm = pe.turn(bank[:, k * P:(k + 1) * P], ho[:, tt, kt * P:(kt + 1) * P])
                        if k == 3:
                            mm.then_inc(to_act.filled, 1)
            pe.wait_ge(xT_ready, pe.due(xT_ready))
            for half in range(2):
                blk = pe.block()
                pe_tok(pe, blk, to_dve, 0, 512, x_lhs)
                pe.used()

        def pe_turn_heads(pe, src):
            for tt in range(2):
                for b in range(2):
                    pe.wait_ge(to_dve.freed, to_dve.next_free())
                    bank = to_dve.free_bank()
                    for j in range(4):
                        o = (4 * b + j) * SEQ + tt * P
                        mm = pe.turn(bank[:, j * P:(j + 1) * P], src[:, o:o + P])
                        if j == 3:
                            mm.then_inc(to_dve.filled, 1)

        def dve_keep_heads(dve, dst):
            d3 = dst.rearrange("p (t n) -> p t n", t=2)
            for tt in range(2):
                for b in range(2):
                    dve.wait_ge(to_dve.filled, to_dve.next_filled())
                    bank = to_dve.filled_bank()
                    ins = nc.vector.tensor_copy(d3[:, tt, 512 * b:512 * b + 512], bank[:])
                    ins.then_inc(to_dve.freed, dve.up(to_dve.freed))
            dve.wait_ge(to_dve.freed, dve.sent(to_dve.freed))

        def act_hgrn(act):
            e = act.e
            def forget(back, k):
                act.wait_ge(to_act.filled, to_act.next_filled())
                bank = to_act.filled_bank()
                ins = e.activation(hz[back][:, :, k], bank[:].rearrange("p (s t) -> p s t", s=2), ACT.Sigmoid)
                ins.then_inc(to_act.freed, act.up(to_act.freed))
                act.wait_ge(to_act.freed, act.sent(to_act.freed))

            def values(half):
                for tt in range(4):
                    act.wait_ge(to_act.filled, to_act.next_filled())
                    bank = to_act.filled_bank()
                    ins = e.copy(hv[:, tt, 512 * half:512 * half + 512], bank[:])
                    ins.then_inc(to_act.freed, act.up(to_act.freed))
                    act.wait_ge(to_act.freed, act.sent(to_act.freed))

            def late_unit(u):
                if u < 8:
                    forget(1, u)
                else:
                    half, tt = (u - 8) // 2, u % 2
                    act.wait_ge(to_act.filled, to_act.next_filled())
                    bank = to_act.filled_bank()
                    ins = e.activation(hgate[:, tt, 512 * half:512 * half + 512], bank[:], ACT.Sigmoid)
                    ins.then_inc(to_act.freed, act.up(to_act.freed))
                    act.wait_ge(to_act.freed, act.sent(to_act.freed))

            def log_forget(back):
                act.wait_ge(forget_ready, act.due(forget_ready))
                e.activation(hz[back][:], hz[back][:], ACT.Ln).then_inc(log_forget_ready, act.up(log_forget_ready))
                act.wait_ge(log_forget_ready, act.sent(log_forget_ready))

            def ctx_decay():
                act.wait_ge(ctx_diff_ready, act.due(ctx_diff_ready))
                e.activation(hQ, hQ, ACT.Exp).then_inc(ctx_decay_ready, act.up(ctx_decay_ready))
                act.wait_ge(ctx_decay_ready, act.sent(ctx_decay_ready))

            for k in range(KT):
                forget(0, k)
            act.sem_inc(hgrn_in_ready, act.up(hgrn_in_ready))
            values(0)
            log_forget(0)
            values(1)
            for gq in range(4):
                act.wait_ge(to_act.filled, to_act.next_filled())
                bank = to_act.filled_bank()
                ins = e.copy(hq[:, 2 * gq:2 * gq + 2], bank[:].rearrange("p (a t) -> p a t", a=2))
                ins.then_inc(to_act.freed, act.up(to_act.freed))
                act.wait_ge(to_act.freed, act.sent(to_act.freed))
            act.sem_inc(hgrn_in_ready, act.up(hgrn_in_ready))
            for back in range(2):
                if back:
                    log_forget(1)
                ctx_decay()
                act_levels(act, hF, 1.0, not back, None if back else late_unit)
                if not back:
                    late_unit(6)
                act.wait_ge(gb_ready, act.due(gb_ready))
                e.activation(hF, flat(hz[back][:, 0]), ACT.Exp).then_inc(act_step, act.up(act_step))
                act.wait_ge(act_step, act.sent(act_step))
                e.activation(hkF, hkF, ACT.Exp).then_inc(gE_ready, act.up(gE_ready))
                act.wait_ge(gE_ready, act.sent(gE_ready))
                if not back:
                    for u_ in range(7, 12):
                        late_unit(u_)
                    act.sem_inc(hgrn_in_ready, act.up(hgrn_in_ready))
            for _ in range(2):
                act_head_std(act)
            for tt in range(2):
                for q in range(2):
                    act.wait_ge(to_act.filled, to_act.next_filled())
                    bank = to_act.filled_bank()
                    ins = e.copy(xT[:, 4 * q:4 * q + 4, tt * P:(tt + 1) * P],
                                                  bank[:].rearrange("p (k t) -> p k t", k=4))
                    ins.then_inc(to_act.freed, act.up(to_act.freed))
                    act.wait_ge(to_act.freed, act.sent(to_act.freed))
            act.sem_inc(xT_ready, act.up(xT_ready))

        def dve_hgrn(dve):
            v = nc.vector
            dve_gate_rows(dve, 1, GT1, (0,), hdiag)
            one_row = ones[:, 0:1].broadcast_to([P, SEQ])
            for back in range(2):
                z = hz[back]
                dve.wait_ge(hgrn_in_ready, dve.due(hgrn_in_ready))
                for k in range(KT):
                    ins = v.tensor_scalar(z[:, :, k], z[:, :, k], omlb[:, k:k + 1], lb[:, k:k + 1], ALU.mult, ALU.add)
                    ins.then_inc(dve_step, dve.up(dve_step))
                dve.wait_ge(dve_step, dve.sent(dve_step))
                ins = v.tensor_scalar(hk[back][1], z[:, 1], -1.0, 1.0, ALU.mult, ALU.add)
                ins.then_inc(dve_step, dve.up(dve_step))
                dve.wait_ge(dve_step, dve.sent(dve_step))
                ins = v.tensor_scalar(hk[back][0], z[:, 0], -1.0, 1.0, ALU.mult, ALU.add)
                ins.then_inc(forget_ready, dve.up(forget_ready))
                dve.wait_ge(forget_ready, dve.sent(forget_ready))
                dve.wait_ge(log_forget_ready, dve.due(log_forget_ready))
                F3 = hF.rearrange("p (k t) -> p k t", k=KT)
                Q3 = hQ.rearrange("p (k t) -> p k t", k=KT)
                for k in range(KT):
                    ins = v.tensor_tensor_scan(F3[:, k], one_row, z[:, 1, k], 0.0, ALU.mult, ALU.add)
                    ins.then_inc(dve_step, dve.up(dve_step))
                dve.wait_ge(dve_step, dve.sent(dve_step))
                if back:
                    v.tensor_tensor(Q3, F3, z[:, 1], ALU.subtract).then_inc(ctx_diff_ready, dve.up(ctx_diff_ready))
                    dve.wait_ge(ctx_diff_ready, dve.sent(ctx_diff_ready))
                else:
                    ins = v.tensor_tensor(Q3, F3[:, :, SEQ - 1:SEQ].broadcast_to([P, KT, SEQ]), F3, ALU.subtract)
                    ins.then_inc(ctx_diff_ready, dve.up(ctx_diff_ready))
                    dve.wait_ge(ctx_diff_ready, dve.sent(ctx_diff_ready))
                dve.wait_ge(ctx_decay_ready, dve.due(ctx_decay_ready))
                if not back:
                    dve.wait_ge(hgrn_in_ready, dve.due(hgrn_in_ready))
                v.tensor_tensor(Q3, Q3, hk[back][1], ALU.mult).then_inc(ctx_keys_ready, dve.up(ctx_keys_ready))
                dve.wait_ge(ctx_keys_ready, dve.sent(ctx_keys_ready))
                dve_keep_heads(dve, hkF)
                dve.sem_inc(key_tok_ready, dve.up(key_tok_ready))
                for b in range(2):
                    dve.wait_ge(to_dve.filled, to_dve.next_filled())
                    bank = to_dve.filled_bank()
                    ins = v.tensor_copy(hS[:, 4 * b:4 * b + 4], bank[:].rearrange("p (h n) -> p h n", h=4))
                    ins.then_inc(to_dve.freed, dve.up(to_dve.freed))
                    dve.wait_ge(to_dve.freed, dve.sent(to_dve.freed))
                for k in range(KT):
                    ins = v.tensor_tensor_scan(F3[:, k], resets, z[:, 0, k], 0.0, ALU.mult, ALU.add)
                    ins.then_inc(dve_step, dve.up(dve_step))
                dve.wait_ge(dve_step, dve.sent(dve_step))
                b = flat(z[:, 0])
                b4 = b.rearrange("p (n t) -> p n t", t=C)
                F4 = hF.rearrange("p (n t) -> p n t", t=C)
                n = KT * SEQ // C
                if back:
                    v.tensor_tensor(hQ.rearrange("p (n t) -> p n t", t=C), F4[:, :, C - 1:C].broadcast_to([P, n, C]),
                                           F4, ALU.subtract).then_inc(dve_step, dve.up(dve_step))
                    dve.wait_ge(dve_step, dve.sent(dve_step))
                    v.tensor_tensor(b, b, hQ, ALU.add).then_inc(dve_step, dve.up(dve_step))
                    dve.wait_ge(dve_step, dve.sent(dve_step))
                else:
                    v.tensor_copy(b, hF).then_inc(dve_step, dve.up(dve_step))
                    dve.wait_ge(dve_step, dve.sent(dve_step))

                q = flat(hq)

                def write_q(h, F):
                    if h is None:
                        v.tensor_copy(hQ, q).then_inc(dve_step, dve.up(dve_step))
                        dve.wait_ge(dve_step, dve.sent(dve_step))
                    else:
                        ins = v.tensor_tensor(halves(hQ, h, not back)[0], halves(q, h, not back)[0],
                                                     halves(F, h, not back)[0], ALU.mult)
                        ins.then_inc(dve_step, dve.up(dve_step))
                        dve.wait_ge(dve_step, dve.sent(dve_step))

                dve_levels(dve, b, q, flat(hk[back][0]), hF, write_q, hkF,
                           [hatt[:, 4 * i:4 * i + 4] for i in range(4)], not back)
                end = 0 if back else C - 1
                v.tensor_tensor(hkF.rearrange("p (n t) -> p n t", t=C), b4[:, :, end:end + 1].broadcast_to([P, n, C]),
                                       b4, ALU.subtract).then_inc(gb_ready, dve.up(gb_ready))
                dve.wait_ge(gb_ready, dve.sent(gb_ready))
                dve.wait_ge(gE_ready, dve.due(gE_ready))
                v.tensor_tensor(hQ, q, hF, ALU.mult).then_inc(dve_step, dve.up(dve_step))
                dve.wait_ge(dve_step, dve.sent(dve_step))
                ins = v.tensor_copy(hend[:].rearrange("p k c -> p (k c)"), F4[:, :, end])
                ins.then_inc(dve_step, dve.up(dve_step))
                dve.wait_ge(dve_step, dve.sent(dve_step))
                v.tensor_tensor(hkF, hkF, flat(hk[back][0]), ALU.mult).then_inc(kend_ready, dve.up(kend_ready))
                dve.wait_ge(kend_ready, dve.sent(kend_ready))
                dve_keep_heads(dve, hF)
                dve.sem_inc(state_ready, dve.up(state_ready))
                for i in range(4):
                    n = 3 - i if back else i
                    tt, c = n // 2, n % 2
                    r_ = slice(64 * c, 64 * c + 64)
                    for b_ in range(2):
                        o = ho[r_, tt, 512 * b_:512 * b_ + 512]
                        dve.wait_ge(to_dve.filled, to_dve.next_filled())
                        bank = to_dve.filled_bank()
                        if back:
                            v.tensor_tensor(o, bank[r_, :], o, ALU.add).then_inc(to_dve.freed, dve.up(to_dve.freed))
                            dve.wait_ge(to_dve.freed, dve.sent(to_dve.freed))
                        else:
                            v.tensor_copy(o, bank[r_, :]).then_inc(to_dve.freed, dve.up(to_dve.freed))
                            dve.wait_ge(to_dve.freed, dve.sent(to_dve.freed))
                    for b_ in range(2):
                        dve.wait_ge(to_dve.filled, to_dve.next_filled())
                        bank = to_dve.filled_bank()
                        for j in range(4):
                            h = 4 * b_ + j
                            ins = v.scalar_tensor_tensor(out=hS[:, h], in0=hS[:, h], scalar=hend[:, h, n:n + 1],
                                                         in1=bank[:, j * P:(j + 1) * P], op0=ALU.mult, op1=ALU.add)
                            if j == 3:
                                ins.then_inc(to_dve.freed, dve.up(to_dve.freed))
                                dve.wait_ge(to_dve.freed, dve.sent(to_dve.freed))
                            else:
                                ins.then_inc(dve_step, dve.up(dve_step))
                                dve.wait_ge(dve_step, dve.sent(dve_step))
                    dve.sem_inc(state_ready, dve.up(state_ready))
            dve.wait_ge(out_norm_landed, dve.due(out_norm_landed, 16))
            for tt in range(2):
                y = ho[:, tt]
                y3 = y.rearrange("p (h n) -> p h n", h=KT)
                dve_head_std(dve, y3, h_tmp.rearrange("p (h n) -> p h n", h=KT), KT, P, HEAD_EPS)
                v.tensor_tensor(y, y, lnp[:, 1], ALU.mult).then_inc(dve_step, dve.up(dve_step))
                dve.wait_ge(dve_step, dve.sent(dve_step))
                v.tensor_tensor(y, y, hgate[:, tt], ALU.mult).then_inc(readout_ready, dve.up(readout_ready))
                dve.wait_ge(readout_ready, dve.sent(readout_ready))
            dve.sem_inc(out_norm_used, dve.up(out_norm_used))
            dve_gated_residual(dve, (0,), hrow_tmp)

        def second_loads(load, wide, ffn):
            wide(a["attn_w_qkv_2"][0], 0, 1536)
            wide(a["attn_w_o_2"][0], 0, D)
            ffn(a["ffn_w_in_2"][0], 0, a["ffn_w_in_2"][0], D_FF, a["ffn_w_out_2"][0])
            w_ = a["hgrn_w_in_2"][0]
            for c0 in (2 * D, 4 * D, 0, 3 * D, D):
                wide(w_, c0, D)
            wide(a["hgrn_w_o_2"][0], 0, D)
            ffn(a["ffn_w_in_2"][1], 0, a["ffn_w_in_2"][1], D_FF, a["ffn_w_out_2"][1])

        def second_pe(pe):
            pe.wait_ge(rows2_landed, pe.due(rows2_landed, 16 * 4))
            pe.wait_ge(to_dve.freed, to_dve.next_free())
            bank = to_dve.free_bank()
            mm = pe.turn(bank[:, 0:P], rows[:])
            mm.then_inc(to_dve.filled, 1)
            pe.wait_ge(lb_rows_landed, pe.due(lb_rows_landed, 16))
            pe.wait_ge(to_dve.freed, to_dve.next_free())
            bank = to_dve.free_bank()
            mm = pe.turn(bank[:, 0:16], rows[0:16, :], 16)
            mm.then_inc(to_dve.filled, 1)
            pe_norm_mod(pe, (0, 1))
            pe_attention(pe)
            pe_norm_mod(pe, (0, 1))
            pe_gate_rows(pe, (0, 1), diag)
            pe_ffn(pe, 512)
            pe_norm_mod(pe, (0, 1))
            pe_hgrn(pe)
            pe_norm_mod(pe, (0,))
            pe_gate_rows(pe, (0,), diag)
            pe_ffn(pe, SEQ)

        def second_act(act):
            act.sem_inc(ada_ready, act.up(ada_ready))
            act.wait_ge(lb_max_ready, act.due(lb_max_ready))
            act.e.activation(lbc[:, 0:16], lbc[:, 0:16], ACT.Exp).then_inc(lb_exp_ready, act.up(lb_exp_ready))
            act.wait_ge(lb_exp_ready, act.sent(lb_exp_ready))
            act_norm_mod(act, 0, 0, (0, 1))
            act_attention(act)
            act_norm_mod(act, 0, 1, (0, 1))
            act_ffn(act, 512)
            act_norm_mod(act, 1, 0, (0, 1))
            act_hgrn(act)
            act_norm_mod(act, 1, 1, (0,))
            act_ffn(act, SEQ)
            act_std(act)

        def dve_parameters(dve):
            v = nc.vector
            dve.wait_ge(to_dve.filled, to_dve.next_filled())
            bank = to_dve.filled_bank()
            v.tensor_copy(cols[:], bank[:, 0:P]).then_inc(to_dve.freed, dve.up(to_dve.freed))
            dve.wait_ge(to_dve.freed, dve.sent(to_dve.freed))
            dve.sem_inc(cols_free, dve.up(cols_free))
            dve.wait_ge(ada_ready, dve.due(ada_ready))
            for l in range(DEPTH):
                b = cols[:, ADA_B + 48 * l:ADA_B + 48 * (l + 1)].unsqueeze(2).broadcast_to([P, 48, 2])
                v.tensor_tensor(mod[:, l], mod[:, l], b, ALU.add).then_inc(dve_step, dve.up(dve_step))
                dve.wait_ge(dve_step, dve.sent(dve_step))
                for w_, (part, col) in enumerate(((SC1, MIX_W), (SC2, FFN_W))):
                    nw = cols[:, col + KT * l:col + KT * (l + 1)].unsqueeze(2).broadcast_to([P, KT, 2])
                    ins = (v.scalar_tensor_tensor(out=Amod[:, l, w_], in0=mod[:, l, part * KT:(part + 1) * KT], scalar=1.0,
                                                        in1=nw, op0=ALU.add, op1=ALU.mult))
                    ins.then_inc(dve_step, dve.up(dve_step))
                    dve.wait_ge(dve_step, dve.sent(dve_step))
            dve.wait_ge(to_dve.filled, to_dve.next_filled())
            bank = to_dve.filled_bank()
            v.tensor_copy(lbc[:, 0:16], bank[:, 0:16]).then_inc(to_dve.freed, dve.up(to_dve.freed))
            dve.wait_ge(to_dve.freed, dve.sent(to_dve.freed))
            m_ = lbc[:, 16:24]
            v.tensor_tensor(m_, lbc[:, 0:8], lbc[:, 8:16], ALU.max).then_inc(dve_step, dve.up(dve_step))
            dve.wait_ge(dve_step, dve.sent(dve_step))
            v.tensor_tensor(lbc[:, 0:8], lbc[:, 0:8], m_, ALU.subtract).then_inc(dve_step, dve.up(dve_step))
            dve.wait_ge(dve_step, dve.sent(dve_step))
            ins = v.tensor_tensor(lbc[:, 8:16], lbc[:, 8:16], m_, ALU.subtract)
            ins.then_inc(lb_max_ready, dve.up(lb_max_ready))
            dve.wait_ge(lb_max_ready, dve.sent(lb_max_ready))
            dve.wait_ge(lb_exp_ready, dve.due(lb_exp_ready))
            v.tensor_tensor(m_, lbc[:, 0:8], lbc[:, 8:16], ALU.add).then_inc(dve_step, dve.up(dve_step))
            dve.wait_ge(dve_step, dve.sent(dve_step))
            v.reciprocal(m_, m_).then_inc(dve_step, dve.up(dve_step))
            dve.wait_ge(dve_step, dve.sent(dve_step))
            v.tensor_tensor(lbc[:, 24:32], lbc[:, 0:8], m_, ALU.mult).then_inc(dve_step, dve.up(dve_step))
            dve.wait_ge(dve_step, dve.sent(dve_step))
            v.tensor_tensor(lbc[:, 16:24], lbc[:, 8:16], m_, ALU.mult).then_inc(dve_step, dve.up(dve_step))
            dve.wait_ge(dve_step, dve.sent(dve_step))
            ins = v.tensor_tensor(lbc[:, 16:24], lbc[:, 16:24], lbc[:, 24:32], ALU.add)
            ins.then_inc(dve_step, dve.up(dve_step))
            dve.wait_ge(dve_step, dve.sent(dve_step))
            v.tensor_tensor(lb, lbc[:, 16:24], lbc[:, 24:32], ALU.subtract).then_inc(dve_step, dve.up(dve_step))
            dve.wait_ge(dve_step, dve.sent(dve_step))
            v.tensor_scalar(omlb, lb, -1.0, 1.0, ALU.mult, ALU.add).then_inc(dve_step, dve.up(dve_step))
            dve.wait_ge(dve_step, dve.sent(dve_step))

        def second_dve(dve):
            v = nc.vector
            dve_parameters(dve)
            dve.wait_ge(ctx_landed, dve.due(ctx_landed, 16))
            dve_norm_mod(dve, (0, 1))
            dve_attention(dve)
            dve_gate_rows(dve, 0, GT2, (0, 1), diag)
            dve_ffn(dve, 512)
            dve_gated_residual(dve, (0, 1), gtmp_row)
            dve.sem_inc(lnp_free, dve.up(lnp_free))
            dve_hgrn(dve)
            dve_gate_rows(dve, 1, GT2, (0,), diag)
            dve_ffn(dve, SEQ)
            dve_gated_residual(dve, (0,), gtmp_row, norm=False)
            dve.wait_ge(final_norm_landed, dve.due(final_norm_landed, 16))
            for tt in range(2):
                dve_rstd(dve, xtok[:, tt], xn[:, 0, tt])
                ins = v.scalar_tensor_tensor(out=xtok[:, tt], in0=xtok[:, tt], scalar=small[:, 4:5], in1=lnp[:, 1],
                                                    op0=ALU.mult, op1=ALU.mult)
                ins.then_inc(result_ready, dve.up(result_ready))
                dve.wait_ge(result_ready, dve.sent(result_ready))

        def second_pool(pool):
            e = pool.e
            pool.wait_ge(cols_free, pool.due(cols_free))
            e.dma_start(rows[0:16, :], a["norm_mix_w_2"].rearrange("l (r p) -> (l r) p", p=P)).then_inc(rows2_landed, 16)
            e.dma_start(rows[16:32, :], a["norm_ffn_w_2"].rearrange("l (r p) -> (l r) p", p=P)).then_inc(rows2_landed, 16)
            for l in range(DEPTH):
                e.dma_start(rows[32 + 48 * l:80 + 48 * l, :], a["ada_b_2"][l].rearrange("(r p) -> r p", p=P)
                            ).then_inc(rows2_landed, 16)
            pool.wait_ge(ln_used, pool.due(ln_used))
            e.dma_start(ctok[:], a["ctx_2"][0].rearrange("(t p) d -> p t d", p=P)).then_inc(ctx_landed, 16)
            pool.wait_ge(cols_free, pool.due(cols_free))
            e.dma_start(rows[0:16, :], a["hgrn_lb_logits_2"].rearrange("l (r p) -> (l r) p", p=P)
                        ).then_inc(lb_rows_landed, 16)
            for j, n in enumerate(("attn_q_norm_2", "attn_k_norm_2")):
                e.dma_start(qkn[:, j], a[n][0:1, :].broadcast_to([P, 64])).then_inc(qk_norm_landed, 16)
            pool.wait_ge(lnp_free, pool.due(lnp_free))
            e.dma_start(lnp[:, 1], a["hgrn_out_norm_2"][0:1, :].broadcast_to([P, D])).then_inc(out_norm_landed, 16)
            pool.wait_ge(out_norm_used, pool.due(out_norm_used))
            e.dma_start(lnp[:, 1], a["final_norm_w_2"].rearrange("(a n) -> a n", a=1).broadcast_to([P, D])
                        ).then_inc(final_norm_landed, 16)

        def first_pe(pe):
            pe_turn_c(pe)
            pe_turn_x(pe, X2)
            pe.wait_ge(c_cols_ready, pe.due(c_cols_ready))
            for l in range(DEPTH):
                pe_ffn(pe, SEQ)
                pe_ada(pe)
                pe_turn_x(pe, X2)
                pe_mix(pe, l)
                pe_ada(pe)
                pe_turn_x(pe, X2)
                pe_ffn(pe, SEQ)
                pe_ada(pe)
                pe_turn_x(pe, X2)
                pe_ple(pe)
                pe_ada(pe)
                if l < DEPTH - 1:
                    pe_turn_x(pe, X2)

        def act_ada_std(act):
            for step, i in ada_steps():
                act_ada(act, step, i)
                if step == "product" and i < 2:
                    act_std(act, 1)

        def first_act(act):
            act_turn_c(act)
            act_turn_x(act, X2)
            for l in range(DEPTH):
                act_ffn(act, SEQ)
                act_ada_std(act)
                act_turn_x(act, X2)
                act_mix(act, l)
                act_ada_std(act)
                act_turn_x(act, X2)
                act_ffn(act, SEQ)
                act_ada_std(act)
                act_turn_x(act, X2)
                act_ple(act)
                act_ada_std(act)
                if l < DEPTH - 1:
                    act_turn_x(act, X2)

        def first_dve(dve):
            dve.wait_ge(x_landed, dve.due(x_landed, 16))
            dve.sem_inc(x_ready, dve.up(x_ready))
            dve.sem_inc(x_ready, dve.up(x_ready))
            dve_scale_x(dve)
            for l in range(DEPTH):
                dve_ffn(dve, SEQ)
                dve_residual(dve, 0.5)
                dve_layer_norm(dve)
                dve_mix(dve, l)
                dve_residual(dve, 1.0)
                dve_layer_norm(dve)
                dve_ffn(dve, SEQ)
                dve_residual(dve, 0.5)
                dve_layer_norm(dve)
                dve_ple(dve)
                dve_layer_norm(dve, last=(l == DEPTH - 1))

        def first_pool(pool):
            e = pool.e
            e.dma_start(cst[:], a["cst"]).then_inc(consts_landed, 16)

            def ln(l, n):
                for j, w in enumerate((a["ln_g"], a["ln_b"])):
                    e.dma_start(lnp[:, j], w[l, n:n + 1, :].broadcast_to([P, D])).then_inc(ln_landed, 16)

            for l in range(DEPTH):
                if l:
                    pool.wait_ge(ln_used, pool.due(ln_used))
                ln(l, 0)
                pool_mix(pool, l)
                for n in range(1, 4):
                    if n > 1:
                        pool.wait_ge(ln_used, pool.due(ln_used))
                    ln(l, n)
                    if n == 2:
                        pool_ple(pool, l)

        @block.sync
        def _(eng):
            sp_program(eng)

        @block.tensor
        def _(eng):
            pe_program(eng)

        @block.scalar
        def _(eng):
            act = Side(eng)
            act.silus = act.gates = act.ada = 0
            act.sem_inc(to_act.freed, act.up(to_act.freed, 4))
            act_first_loads(act)
            act.wait_ge(consts_landed, act.due(consts_landed, 16))
            first_act(act)
            second_act(act)

        @block.vector
        def _(eng):
            dve = Side(eng)
            dve.silus = 0
            dve.sem_inc(to_dve.freed, dve.up(to_dve.freed, 4))
            dve.sem_inc(silu_used, dve.up(silu_used, 2))
            dve.wait_ge(consts_landed, dve.due(consts_landed, 16))
            first_dve(dve)
            second_dve(dve)

        @block.gpsimd
        def _(eng):
            pool = Side(eng)
            first_pool(pool)
            second_pool(pool)


NAMES = ["x", "p", "ln_g", "ln_b", "ffn_w1", "ffn_w3", "ffn_w2", "w_in", "rw_mu", "rw_w0", "rw_w2", "rw_a0", "rw_a2",
         "rw_g2", "rw_k_k", "rw_k_a", "rw_r_k", "rw_gn_g", "rw_gn_b", "gla_gk_w2", "gla_gk_b", "gla_norm_g",
         "gdn_conv_w", "gdn_a_log", "gdn_dt_bias", "gdn_norm_g", "w_branch", "w_o", "ple_w_gate", "ple_w_proj", "c_2",
         "ctx_2", "c_ctx_2", "ada_w_2", "ada_b_2", "norm_mix_w_2", "norm_ffn_w_2", "attn_w_qkv_2", "attn_q_norm_2",
         "attn_k_norm_2", "attn_w_o_2", "hgrn_w_in_2", "hgrn_lb_logits_2", "hgrn_out_norm_2", "hgrn_w_o_2",
         "ffn_w_in_2", "ffn_w_out_2", "final_norm_w_2"]


def kernel(**inputs):
    import concourse.bacc as bacc
    from concourse.bass_utils import run_bass_kernel_spmd

    nc = bacc.Bacc("TRN2", target_bir_lowering=False, num_devices=1)
    arrays, aps = {}, {}
    for name in NAMES + ["cst"]:
        arr = CST if name == "cst" else np.ascontiguousarray(inputs[name])
        arrays["in_" + name] = arr
        aps[name] = nc.dram_tensor("in_" + name, arr.shape, mybir.dt.from_np(arr.dtype), kind="ExternalInput").ap()
    out = nc.dram_tensor("out_y", (1, SEQ, D), F32, kind="ExternalOutput").ap()
    two_blocks(nc, aps, out)
    return run_bass_kernel_spmd(nc, [arrays], core_ids=[0]).results[0]["out_y"]
```
